# Optimizing a Trainium2 kernel written in Bass

```python
import jax, jax.numpy as jnp
from jax import lax
import numpy as np

D_MODEL = 2048
BATCH = 1
SEQ = 512
DEPTH = 1

HEAD_DIM = 128
ATTN_HEADS = 8
ATTN_KV_HEADS = 2
ATTN_WIDTH = ATTN_HEADS * HEAD_DIM
KV_WIDTH = ATTN_KV_HEADS * HEAD_DIM
DN_HEADS = 8
DN_KEY_DIM = 128
DN_VAL_DIM = 128
DN_KEY_WIDTH = DN_HEADS * DN_KEY_DIM
DN_VAL_WIDTH = DN_HEADS * DN_VAL_DIM
MIX_WIDTH = ATTN_WIDTH + DN_VAL_WIDTH
N_DIR = 2
DN_QKV_WIDTH = 2 * DN_KEY_WIDTH + DN_VAL_WIDTH
IN_WIDTH = ATTN_WIDTH + 2 * KV_WIDTH + DN_QKV_WIDTH + DN_VAL_WIDTH + 2 * N_DIR * DN_HEADS
SHORT_CONV = 3
FFN_CONV = 3
D_FF = 5632
GRID_W = 64
ROPE_THETA = 10000.0
Q_BLOCK = 128
DN_CHUNK = 64
NORM_EPS = 1e-6
N_MOD = 6

kernel_name = "hymba_axial_gqa_gated_deltanet_convffn_adaln"

def rms_norm(x, eps=NORM_EPS):
    x32 = x.astype(jnp.float32)
    return (x32 * lax.rsqrt(jnp.mean(x32 * x32, axis=-1, keepdims=True) + eps)).astype(x.dtype)

def l2_normalize(x, eps=NORM_EPS):
    return x * lax.rsqrt(jnp.sum(x * x, axis=-1, keepdims=True) + eps)

def modulated_rms_norm(x, shift, scale):
    return rms_norm(x) * (1.0 + scale[:, None, :]) + shift[:, None, :]

def dwconv_centred(x, w):
    K = w.shape[0]
    pad = K // 2
    S = x.shape[1]
    xp = jnp.pad(x, ((0, 0), (pad, pad), (0, 0)))
    out = xp[:, 0:S] * w[0]
    for j in range(1, K):
        out = out + xp[:, j:j + S] * w[j]
    return out

def axial_rope_tables(S, dtype):
    rows = S // GRID_W
    row_ids = jnp.repeat(jnp.arange(rows, dtype=jnp.int32), GRID_W)
    col_ids = jnp.tile(jnp.arange(GRID_W, dtype=jnp.int32), rows)
    axis_dim = HEAD_DIM // 2
    inv_freq = ROPE_THETA ** (-jnp.arange(0, axis_dim, 2, dtype=jnp.float32) / axis_dim)
    ang_r = row_ids.astype(jnp.float32)[:, None] * inv_freq
    ang_c = col_ids.astype(jnp.float32)[:, None] * inv_freq
    return (jnp.cos(ang_r).astype(dtype), jnp.sin(ang_r).astype(dtype),
            jnp.cos(ang_c).astype(dtype), jnp.sin(ang_c).astype(dtype))

def rope_rotate(x, cos, sin):
    x1, x2 = jnp.split(x, 2, axis=-1)
    return jnp.concatenate([x1 * cos - x2 * sin, x2 * cos + x1 * sin], axis=-1)

def apply_axial_rope(x, cos_r, sin_r, cos_c, sin_c):
    half = HEAD_DIM // 2
    return jnp.concatenate([rope_rotate(x[..., :half], cos_r, sin_r),
                            rope_rotate(x[..., half:], cos_c, sin_c)], axis=-1)

def axial_gqa_attention(q, k, v, q_gain, k_gain):
    B, S = q.shape[0], q.shape[1]
    q = (rms_norm(q) * q_gain).transpose(0, 2, 1, 3)
    k = (rms_norm(k) * k_gain).transpose(0, 2, 1, 3)
    v = v.transpose(0, 2, 1, 3)
    tables = axial_rope_tables(S, q.dtype)
    q = apply_axial_rope(q, *tables)
    k = apply_axial_rope(k, *tables)
    G = ATTN_HEADS // ATTN_KV_HEADS
    nb = S // Q_BLOCK
    qb = q.reshape(B, ATTN_KV_HEADS, G, nb, Q_BLOCK, HEAD_DIM).transpose(3, 0, 1, 2, 4, 5)
    scale = HEAD_DIM ** -0.5

    def attend(q_blk):
        s = jnp.einsum('bhgqd,bhkd->bhgqk', q_blk, k,
                       preferred_element_type=jnp.float32) * scale
        p = jax.nn.softmax(s, axis=-1).astype(v.dtype)
        return jnp.einsum('bhgqk,bhkd->bhgqd', p, v)

    o = lax.map(attend, qb)
    return o.transpose(1, 0, 4, 2, 3, 5).reshape(B, S, ATTN_WIDTH)

def gated_delta_chunked(q, k, v, beta, g):
    B, H, S, dk = q.shape
    dv = v.shape[-1]
    C = DN_CHUNK
    N = S // C
    q = q.reshape(B, H, N, C, dk)
    k = k.reshape(B, H, N, C, dk)
    v = v.reshape(B, H, N, C, dv)
    beta = beta.reshape(B, H, N, C)
    gc = jnp.cumsum(g.reshape(B, H, N, C), axis=-1)
    tril = jnp.tril(jnp.ones((C, C), dtype=bool))
    strict = jnp.tril(jnp.ones((C, C), dtype=bool), -1)
    diff = gc[..., :, None] - gc[..., None, :]
    decay = jnp.where(tril, jnp.exp(jnp.where(tril, diff, 0.0)), 0.0)
    kb = k * beta[..., None]
    vb = v * beta[..., None]
    L = jnp.where(strict, jnp.einsum('bhncd,bhnjd->bhncj', kb, k) * decay, 0.0)
    A = L + jnp.eye(C, dtype=L.dtype)
    rhs = jnp.concatenate([vb, kb * jnp.exp(gc)[..., None]], axis=-1)
    sol = lax.linalg.triangular_solve(A, rhs, left_side=True, lower=True, unit_diagonal=True)
    u = sol[..., :dv]
    w = sol[..., dv:]
    qk = jnp.where(tril, jnp.einsum('bhncd,bhnjd->bhncj', q, k) * decay, 0.0)
    q_dec = q * jnp.exp(gc)[..., None]
    k_dec = k * jnp.exp(gc[..., -1:] - gc)[..., None]
    g_last = jnp.exp(gc[..., -1])

    def step(state, inp):
        qk_i, qd_i, kd_i, u_i, w_i, gl_i = inp
        v_new = u_i - jnp.einsum('bhcd,bhde->bhce', w_i, state)
        o = (jnp.einsum('bhcd,bhde->bhce', qd_i, state)
             + jnp.einsum('bhcj,bhje->bhce', qk_i, v_new))
        state = state * gl_i[..., None, None] + jnp.einsum('bhcd,bhce->bhde', kd_i, v_new)
        return state, o

    xs = tuple(jnp.moveaxis(t, 2, 0) for t in (qk, q_dec, k_dec, u, w, g_last))
    state0 = jnp.zeros((B, H, dk, dv), dtype=jnp.float32)
    _, o = lax.scan(step, state0, xs)
    return jnp.moveaxis(o, 0, 2).reshape(B, H, S, dv)

def bidir_gated_deltanet(qkv, z, b_raw, a_raw, conv_w, A_log, dt_bias, norm_w):
    B, S = qkv.shape[0], qkv.shape[1]
    qkv = jax.nn.silu(dwconv_centred(qkv, conv_w)).astype(jnp.float32)
    q, k, v = jnp.split(qkv, [DN_KEY_WIDTH, 2 * DN_KEY_WIDTH], axis=-1)
    q = (l2_normalize(q.reshape(B, S, DN_HEADS, DN_KEY_DIM)) * DN_KEY_DIM ** -0.5).transpose(0, 2, 1, 3)
    k = l2_normalize(k.reshape(B, S, DN_HEADS, DN_KEY_DIM)).transpose(0, 2, 1, 3)
    v = v.reshape(B, S, DN_HEADS, DN_VAL_DIM).transpose(0, 2, 1, 3)
    beta = jax.nn.sigmoid(b_raw.astype(jnp.float32)).reshape(B, S, N_DIR, DN_HEADS)
    g = -jnp.exp(A_log.astype(jnp.float32)) * jax.nn.softplus(
        a_raw.astype(jnp.float32).reshape(B, S, N_DIR, DN_HEADS) + dt_bias.astype(jnp.float32))
    beta = beta.transpose(2, 0, 3, 1)
    g = g.transpose(2, 0, 3, 1)
    o_fwd = gated_delta_chunked(q, k, v, beta[0], g[0])
    flip = lambda t: jnp.flip(t, axis=2)
    o_bwd = flip(gated_delta_chunked(flip(q), flip(k), flip(v), flip(beta[1]), flip(g[1])))
    o = (o_fwd + o_bwd).transpose(0, 2, 1, 3)
    gate = jax.nn.silu(z.astype(jnp.float32).reshape(B, S, DN_HEADS, DN_VAL_DIM))
    o = rms_norm(o) * norm_w.astype(jnp.float32) * gate
    return o.reshape(B, S, DN_VAL_WIDTH).astype(z.dtype)

def in_proj_split_points():
    sizes = [ATTN_WIDTH, KV_WIDTH, KV_WIDTH, DN_QKV_WIDTH, DN_VAL_WIDTH, N_DIR * DN_HEADS]
    points = []
    total = 0
    for s_ in sizes:
        total += s_
        points.append(total)
    return points

def setup_inputs(seed: int = 0) -> dict:
    key = jax.random.key(seed)
    ks = jax.random.split(key, 17)
    f32 = jnp.float32
    nrm = lambda k_, shape, s: jax.random.normal(k_, shape, f32) * s
    x = jax.random.normal(ks[0], (BATCH, SEQ, D_MODEL), f32)
    c = jax.random.normal(ks[1], (BATCH, D_MODEL), f32)
    w_ada = nrm(ks[2], (DEPTH, D_MODEL, N_MOD * D_MODEL), D_MODEL ** -0.5)
    b_ada = nrm(ks[3], (DEPTH, N_MOD * D_MODEL), 0.02)
    w_in = nrm(ks[4], (DEPTH, D_MODEL, IN_WIDTH), D_MODEL ** -0.5)
    attn_q_norm = 1.0 + nrm(ks[5], (DEPTH, HEAD_DIM), 0.02)
    attn_k_norm = 1.0 + nrm(ks[6], (DEPTH, HEAD_DIM), 0.02)
    dn_conv_w = nrm(ks[7], (DEPTH, SHORT_CONV, DN_QKV_WIDTH), SHORT_CONV ** -0.5)
    dn_A_log = jnp.log(jax.random.uniform(ks[8], (DEPTH, N_DIR, DN_HEADS), f32, 1.0, 16.0))
    dt = jnp.exp(jax.random.uniform(ks[9], (DEPTH, N_DIR, DN_HEADS), f32,
                                    float(np.log(1e-3)), float(np.log(1e-1))))
    dn_dt_bias = dt + jnp.log(-jnp.expm1(-dt))
    dn_norm_w = 1.0 + nrm(ks[10], (DEPTH, DN_VAL_DIM), 0.02)
    w_out = nrm(ks[11], (DEPTH, MIX_WIDTH, D_MODEL), MIX_WIDTH ** -0.5)
    w_up = nrm(ks[12], (DEPTH, D_MODEL, 2 * D_FF), D_MODEL ** -0.5)
    w_ffn_conv = nrm(ks[13], (DEPTH, FFN_CONV, 2 * D_FF), FFN_CONV ** -0.5)
    b_ffn_conv = nrm(ks[14], (DEPTH, 2 * D_FF), 0.02)
    w_down = nrm(ks[15], (DEPTH, D_FF, D_MODEL), D_FF ** -0.5)
    final_norm = 1.0 + nrm(ks[16], (D_MODEL,), 0.02)
    return {"x": x, "c": c, "w_ada": w_ada, "b_ada": b_ada, "w_in": w_in,
            "attn_q_norm": attn_q_norm, "attn_k_norm": attn_k_norm, "dn_conv_w": dn_conv_w,
            "dn_A_log": dn_A_log, "dn_dt_bias": dn_dt_bias, "dn_norm_w": dn_norm_w,
            "w_out": w_out, "w_up": w_up, "w_ffn_conv": w_ffn_conv, "b_ffn_conv": b_ffn_conv,
            "w_down": w_down, "final_norm": final_norm}

def reference(x, c, w_ada, b_ada, w_in, attn_q_norm, attn_k_norm, dn_conv_w, dn_A_log,
              dn_dt_bias, dn_norm_w, w_out, w_up, w_ffn_conv, b_ffn_conv, w_down, final_norm):
    B, S = x.shape[0], x.shape[1]
    cond = jax.nn.silu(c)
    split_points = in_proj_split_points()
    h = x
    for l in range(DEPTH):
        mod = cond @ w_ada[l] + b_ada[l]
        sh1, sc1, gt1, sh2, sc2, gt2 = jnp.split(mod, N_MOD, axis=-1)
        hn = modulated_rms_norm(h, sh1, sc1)
        proj = hn @ w_in[l]
        aq, ak, av, dqkv, dz, db, da = jnp.split(proj, split_points, axis=-1)
        attn_out = axial_gqa_attention(
            aq.reshape(B, S, ATTN_HEADS, HEAD_DIM),
            ak.reshape(B, S, ATTN_KV_HEADS, HEAD_DIM),
            av.reshape(B, S, ATTN_KV_HEADS, HEAD_DIM),
            attn_q_norm[l], attn_k_norm[l])
        dn_out = bidir_gated_deltanet(dqkv, dz, db, da, dn_conv_w[l], dn_A_log[l],
                                      dn_dt_bias[l], dn_norm_w[l])
        mixed = jnp.concatenate([attn_out, dn_out], axis=-1) @ w_out[l]
        h = h + gt1[:, None, :] * mixed
        hn = modulated_rms_norm(h, sh2, sc2)
        u = dwconv_centred(hn @ w_up[l], w_ffn_conv[l]) + b_ffn_conv[l]
        u_gate, u_val = jnp.split(u, 2, axis=-1)
        h = h + gt2[:, None, :] * ((jax.nn.silu(u_gate) * u_val) @ w_down[l])
    return rms_norm(h) * final_norm


_drawn_inputs = setup_inputs


def setup_inputs(seed=0):
    import zlib

    import numpy as np

    out = dict(_drawn_inputs(seed))
    spreads = {}
    factors = {'attn_q_norm': 8.0,
     'attn_k_norm': 8.0,
     'dn_norm_w': 7.012,
     'b_ffn_conv': 4.912,
     'final_norm': 2.906}
    for name, (base, spread) in spreads.items():
        noise = np.random.default_rng([zlib.crc32(name.encode()), seed]).standard_normal(out[name].shape)
        drawn = base * np.exp(spread * noise) if base else spread * noise
        out[name] = __import__('jax').numpy.asarray(drawn.astype(out[name].dtype))
    for name, factor in factors.items():
        out[name] = (out[name] * factor).astype(out[name].dtype)
    return out
```

```python
from contextlib import ExitStack

import concourse.bass as bass
from concourse import mybir

ALU = mybir.AluOpType
ACT = mybir.ActivationFunctionType
AX = mybir.AxisListType
F32 = mybir.dt.float32
F32R = mybir.dt.float32r
BF16 = mybir.dt.bfloat16

P = 128
S = 512
DM = 2048
KT = DM // P
NB = S // P
HEADS = 8
KV_HEADS = 2
DFF = 5632
FT = DFF // P
CHUNKS = 4
FC = FT // CHUNKS
DN = 64
NCH = S // DN
EPS = 1e-6
BIG = 1e30
UK = 8
ADA_W = 1024
ADA_SLOTS = 4
ADA_STEPS = 6 * DM // ADA_W

COL_QA, COL_KA, COL_VA = 0, 1024, 1280
COL_Q, COL_K, COL_V, COL_Z, COL_BA = 1536, 2560, 3584, 4608, 5632

C_ID, C_ONE, C_ROT = 0, 128, 256
C_CUM, C_REST = 384, 640
C_ML, C_MQ = 896, 1152
C_COS, C_SIN = 1408, 1920
C_EPS = 2432
C_ZERO = 2434
C_N = 2436
SOFT_MAX = [2, 4, 8, 12]
SOFT_OUT = [6, 10, 14, 16]
LEVELS = 6

V_BADA, V_QN, V_KN, V_DNW, V_FN = 0, 96, 97, 98, 99
V_CONV = 115
V_FCONV = V_CONV + 72
V_FB = V_FCONV + 264
V_C = V_FB + 88
V_N = V_C + 16


def shape_constants(np):
    c = np.zeros((P, C_N), np.float32)
    p, f = np.arange(P)[:, None], np.arange(P)[None, :]
    same = p // DN == f // DN
    c[:, C_ID:C_ID + P] = p == f
    c[:, C_ONE:C_ONE + P] = 1.0
    quarter = P // 4
    c[:, C_ROT:C_ROT + P] = ((f // quarter) % 2 == 1) & (p == f - quarter)
    c[:, C_ROT:C_ROT + P] -= ((f // quarter) % 2 == 0) & (p == f + quarter)
    for d, (upto, after) in enumerate(((p <= f, p > f), (p >= f, p < f))):
        c[:, C_CUM + d * P:C_CUM + (d + 1) * P] = same & upto
        c[:, C_REST + d * P:C_REST + (d + 1) * P] = same & after
        c[:, C_ML + d * P:C_ML + (d + 1) * P] = np.where(same & after, 0.0, BIG)
        c[:, C_MQ + d * P:C_MQ + (d + 1) * P] = np.where(same & upto, 0.0, BIG)
    t = np.arange(S)
    inv = (np.float32(10000.0) ** (-np.arange(0, P // 2, 2, dtype=np.float32) / np.float32(P // 2))).astype(np.float32)
    for half, where in enumerate((t // 64, t % 64)):
        angle = where.astype(np.float32)[None, :] * inv[:, None]
        for q in range(2):
            rows = slice(half * 64 + q * 32, half * 64 + q * 32 + 32)
            c[rows, C_COS:C_COS + S] = np.cos(angle)
            c[rows, C_SIN:C_SIN + S] = np.sin(angle)
    c[:, C_EPS] = EPS
    c[:, C_EPS + 1] = EPS * P
    m = np.zeros((P, LEVELS, 2, P), np.float32)
    for n in range(LEVELS):
        b = 1 << n
        pair = p // (2 * b) == f // (2 * b)
        m[:, n, 0] = pair & ((p // b) % 2 == 1) & ((f // b) % 2 == 0)
        m[:, n, 1] = pair & ((p // b) % 2 == 0) & ((f // b) % 2 == 1)
    return c, m.reshape(P, -1)


class Signal:

    def __init__(self, sem, per):
        self.sem, self.per = sem, per

    def after(self, i, k=None):
        return self.sem, i * self.per + (self.per if k is None else k)


def build(nc, A, out):
    ctx = ExitStack()
    with ctx:
        def sb(name, shape, dt=F32, where=ctx):
            return where.enter_context(nc.sbuf_tensor(name, shape, dt))

        def sem(name):
            return ctx.enter_context(nc.semaphore(name))

        def signal(name, per=1):
            return Signal(sem(name), per)

        act_hi = sb("act_hi", [P, KT, S], F32R)
        act_lo = sb("act_lo", [P, KT, S], F32R)
        raw = [sb(f"raw{i}", [P, UK, P]) for i in range(2)]
        w_hi = [sb(f"w_hi{i}", [P, UK, P], F32R) for i in range(2)]
        w_lo = [sb(f"w_lo{i}", [P, UK, P], F32R) for i in range(2)]
        cst = sb("cst_sb", [P, C_N])
        col = sb("col", [P, V_N])
        mod = sb("mod", [P, 6 * KT])
        cond = sb("cond", [P, KT])
        nrm = sb("nrm", [P, 3, NB])

        mixer = ExitStack()
        mixed = sb("mixed", [P, 2 * HEADS, S], F32, mixer)
        ada_w = [sb(f"ada_w{i}", [P, ADA_W], F32, mixer) for i in range(2)]
        ada_acc = sb("ada_acc", [P, ADA_W], F32, mixer)
        lvl = sb("lvl", [P, LEVELS, 2, P], BF16, mixer)
        pre = sb("pre", [P, 3, S + 2], F32, mixer)
        act3 = sb("act3", [P, 3, S], F32, mixer)
        tmp = sb("tmp", [P, 2, S], F32, mixer)
        ktok = sb("ktok", [P, NB, P], F32, mixer)
        vtok = sb("vtok", [P, NB, P], F32, mixer)
        LL = sb("LL", [P, 2, NB, P], F32, mixer)
        DQ = sb("DQ", [P, 2, NB, P], F32, mixer)
        EG = sb("EG", [P, 2, S], F32, mixer)
        TT = sb("TT", [P, 2, NB, P], F32, mixer)
        T = sb("T", [P, 2, NB, P], F32, mixer)
        YL = sb("YL", [P, 2, 2, NB, P], F32, mixer)
        ka = sb("ka", [P, KV_HEADS, S], F32, mixer)
        va = sb("va", [P, KV_HEADS, S], F32, mixer)
        vn = sb("vn", [P, 2, P], F32, mixer)
        st = sb("st", [P, 2, P], F32, mixer)
        gall = sb("gall", [P, 5, NB, 2, HEADS], F32, mixer)
        gcur = sb("gcur", [P, 5, NB, 2], F32, mixer)
        glast = sb("glast", [P, 2, NCH], F32, mixer)
        soft = sb("soft", [P, 4, NB], F32, mixer)
        gates = sb("gates", [P, 2, 16], F32, mixer)
        mixer.close()
        two = lambda t: t[:].rearrange("p d b n -> p (d b n)")
        LLf, DQf, TTf, Tf = two(LL), two(DQ), two(TT), two(T)
        EGf = EG[:].rearrange("p d n -> p (d n)")
        Yf = YL[:, 0].rearrange("p d b n -> p (d b n)")
        LMf = YL[:, 1].rearrange("p d b n -> p (d b n)")
        LM = YL[:, 1]
        ktf = ktok[:].rearrange("p b n -> p (b n)")
        vtf = vtok[:].rearrange("p b n -> p (b n)")
        tmpf = tmp[:].rearrange("p d n -> p (d n)")
        mixedf = mixed[:].rearrange("p t n -> p (t n)")
        qr, vcur = TTf[:, 0:S], TTf[:, S:2 * S].rearrange("p (b n) -> p b n", n=P)
        prob = [Tf[:, 0:S], Tf[:, S:2 * S]]
        sqa, rotsin = Yf[:, 0:S], Yf[:, S:2 * S]
        PT = YL[:].rearrange("p a d b n -> p (a d b n)").rearrange("p (k q) -> p k q", q=S)
        x_in = mixed[:].rearrange("p t n -> p (t n)").rearrange("p (b n) -> p b n", n=DM)
        wba = Tf[:, 0:512].rearrange("p (k n) -> p k n", n=32)
        ada_first = [LLf, DQf, EGf, TTf]
        junk = YL[:].rearrange("p a d b n -> p (a d b n)")
        rows = pre[:].rearrange("p t n -> p (t n)")[:, 0:6 * P].rearrange("p (t n) -> p t n", n=P)
        arow = vn[0:1, 0, 0:32]
        lvl_f32 = [ktf, vtf, act3[:, 1, :]]
        hn_tmp = [tmp[:, 0, :], tmp[:, 1, :]]

        mlp = ExitStack()
        mh_hi = sb("mh_hi", [P, FC, S], F32R, mlp)
        mh_lo = sb("mh_lo", [P, FC, S], F32R, mlp)
        hT = sb("hT", [P, KT, S], F32, mlp)
        sqacc = sb("sqacc", [P, S], F32, mlp)
        sq = sb("sq", [P, S], F32, mlp)
        rstd = sb("rstd", [P, S], F32, mlp)
        gp = sb("gp", [P, 2, S + 2], F32, mlp)
        cv = sb("cv", [P, 2, S], F32, mlp)
        prod = sb("prod", [P, S], F32, mlp)
        hn2 = sb("hn2", [P, 2, S], F32, mlp)
        mlp.close()
        xtok = ctx.enter_context(nc.sbuf_tensor("xtok", [P, NB, DM], F32))
        otok = xtok
        hTf = hT[:].rearrange("p t n -> p (t n)")
        mhf_hi = mh_hi[:].rearrange("p t n -> p (t n)")
        mhf_lo = mh_lo[:].rearrange("p t n -> p (t n)")

        pw = [ctx.enter_context(nc.psum_tensor(f"pw{i}", [P, S], F32)) for i in range(2)]
        pdt = ctx.enter_context(nc.psum_tensor("pd", [P, 6, S], F32))
        pd = [pdt[:, i, :] for i in range(6)]
        pd01 = pdt[:, 0:2, :].rearrange("p a n -> p (a n)")
        pd23 = pdt[:, 2:4, :].rearrange("p a n -> p (a n)")
        pd34 = pdt[:, 3:5, :].rearrange("p a n -> p (a n)")
        pd45 = pdt[:, 4:6, :].rearrange("p a n -> p (a n)")
        ident = cst[:, C_ID:C_ID + P]
        ones = cst[:, C_ONE:C_ONE + P]
        rot = cst[:, C_ROT:C_ROT + P]
        cosT, sinT = cst[:, C_COS:C_COS + S], cst[:, C_SIN:C_SIN + S]
        eps1, eps128 = cst[:, C_EPS:C_EPS + 1], cst[:, C_EPS + 1:C_EPS + 2]

        w_in, w_out, w_up, w_down = A["w_in"][0], A["w_out"][0], A["w_up"][0], A["w_down"][0]

        KV0, HEAD0 = 0, 8
        OUT0 = HEAD0 + 10 * HEADS
        MLP0 = OUT0 + 2 * KT
        MLP_PER = 4 * FC + 2 * KT
        raw_in = [sem(f"raw_in{i}") for i in range(2)]
        hi_made = signal("hi_made")
        lo_made = signal("lo_made")
        unit_used = signal("unit_used")
        tile_taken = signal("tile_taken")
        out_taken = signal("out_taken")
        up_taken = signal("up_taken")

        consts_in, x_loaded, rows_in = sem("consts_in"), sem("x_loaded"), sem("rows_in")
        x2_loaded, stored, ba_in, small_in = sem("x2_loaded"), sem("stored"), sem("ba_in"), sem("small_in")
        lvl_in = [sem(f"lvl_in{i}") for i in range(3)]
        ada_in0 = [sem(f"ada_first_in{i}") for i in range(4)]
        ada_in = [sem(f"ada_in{i}") for i in range(2)]
        ada_step = signal("ada_step", KT)
        ada_sum = signal("ada_sum")
        ada_out = signal("ada_out")

        block = ctx.enter_context(nc.Block())

        conv_step = signal("conv_step", 9)
        gcur_made = signal("gcur_made", 1)
        gu_made = signal("gu_made", 2)
        diff_made = signal("diff_made", 2)
        dq_masked = signal("dq_masked", 1)
        ll_masked = signal("ll_masked", 1)
        norm_made = signal("norm_made", 3)
        rot_scaled = signal("rot_scaled", 1)
        rope_step = signal("rope_step", 2)
        ll_step = signal("ll_step", 2)
        qk_made = signal("qk_made", 1)
        soft_step = signal("soft_step", 4 * NB)
        av_taken = signal("av_taken", 1)
        t_first = signal("t_first", 2)
        t_step = signal("t_step", 9)
        tb_made = signal("tb_made", 2)
        wt_taken = signal("wt_taken", 1)
        kd_made = signal("kd_made", 1)
        gl_made = signal("gl_made", 2)
        qd_made = signal("qd_made", 1)
        vnew_made = signal("vnew_made", 2 * (NCH - 1))
        state_made = signal("state_made", 2 * (NCH - 1))
        o_summed = signal("o_summed", 1)
        mix_step = signal("mix_step", 2)
        silu_done = signal("silu_done", 4)
        sq_done = signal("sq_done", 3)
        eg_done = signal("eg_done", 1)
        ln_done = signal("ln_done", 3)
        rstd_made = signal("rstd_made", 3)
        decay_done = signal("decay_done", 2)
        tok_done = signal("tok_done", 2)
        p_exp = signal("p_exp", NB)
        pt_taken = signal("pt_taken", NB)
        y_taken = signal("y_taken", LEVELS - 1)
        u_taken = signal("u_taken", 1)
        o_taken = signal("o_taken", 1)
        onorm = signal("onorm", 3)
        gc_sum = signal("gc_sum", 2)
        ss_sum = signal("ss_sum", 3)
        tr_sum = signal("tr_sum", 2)
        g_sum = signal("g_sum", 1)
        qk_sum = signal("qk_sum", 1)
        rot_sum = signal("rot_sum", 1)
        sc_sum = signal("sc_sum", NB)
        pt_sum = signal("pt_sum", NB)
        av_sum = signal("av_sum", 1)
        lt_sum = signal("lt_sum", 1)
        y_sum = signal("y_sum", LEVELS - 1)
        a_sum = signal("a_sum", 9)
        u_sum = signal("u_sum", 1)
        wt_sum = signal("wt_sum", 1)
        vn_sum = signal("vn_sum", 2 * (NCH - 1))
        s_sum = signal("s_sum", 2 * (NCH - 1))
        o_sum = signal("o_sum", 2)
        sso_sum = signal("sso_sum", 1)
        lm_made = signal("lm_made", LEVELS)
        vcur_made = signal("vcur_made", 1)

        cols_sum, cols_made, cond_made = signal("cols_sum"), signal("cols_made", 2), signal("cond_made")
        gate_row_sum, gates_made = signal("gate_row_sum"), signal("gates_made", 2)
        x_squared, x_rstd = signal("x_squared", NB), signal("x_rstd", 2)
        x_normed, xt_sum = signal("x_normed", NB), signal("xt_sum", KT)
        hn_full, hn_hi, hn_lo = signal("hn_full", KT), signal("hn_hi", KT), signal("hn_lo", KT)
        lvl_made, pads_made = signal("lvl_made", 3), signal("pads_made", 2)
        scale_made = signal("scale_made")
        ba_sum, cum_sum = signal("ba_sum"), signal("cum_sum")
        gate_a, gate_v = signal("gate_a", 6), signal("gate_v", 7)
        kv_sq, kv_ss, kv_rstd = signal("kv_sq", 1), signal("kv_ss", 1), signal("kv_rstd", 2)
        kv_step, kv_rot = signal("kv_step", 4), signal("kv_rot", 1)
        v_tr, v_tok = signal("v_tr", 1), signal("v_tok", 1)

        mx_hi, mx_lo = signal("mx_hi", KT), signal("mx_lo", KT)
        x2_sum, x2_taken = signal("x2_sum", KT), signal("x2_taken", KT)
        sq_made, sq_added = signal("sq_made", KT), signal("sq_added", KT)
        ssum, rstd_step, scale2_made = signal("ssum"), signal("rstd_step", 2), signal("scale2_made")
        sqacc_step = signal("sqacc_step")
        h2_step, h2_hi, h2_lo = signal("h2_step", 2 * KT), signal("h2_hi", KT), signal("h2_lo", KT)
        fconv_step = signal("fconv_step", 6)
        fsilu, fprod = signal("fsilu"), signal("fprod")
        mh_hi_made, mh_lo_made = signal("mh_hi_made"), signal("mh_lo_made")
        fin_made, fin_sum, fin_taken = signal("fin_made", KT), signal("fin_sum", KT), signal("fin_taken", KT)

        SCALE = float(P) ** -0.5
        TAPS = 3

        @block.sync
        def _(sp):
            sp.dma_start(cst[:], A["shape_constants"]).then_inc(consts_in, 16)
            for b in range(NB):
                sp.dma_start(x_in[:, b, :], A["x"][0, b * P:(b + 1) * P, :]).then_inc(x_loaded, 16)
            sp.dma_start(wba, w_in[:, COL_BA:COL_BA + 32].rearrange("(k p) n -> p k n", p=P)).then_inc(ba_in, 16)

            def load(slot, u, src, n_k, first=False):
                if not first:
                    sp.wait_ge(lo_made.sem, u - 1)
                sp.dma_start(raw[slot][:, 0:n_k, :], src.rearrange("(k p) n -> p k n", p=P)).then_inc(raw_in[slot], 16)

            def tile(u, w, column, first=False):
                for j in range(2):
                    load(j, u + j, w[j * UK * P:(j + 1) * UK * P, bass.ds(column, P)], UK, first)

            for t, c0 in enumerate((COL_KA, COL_KA + P, COL_VA, COL_VA + P)):
                tile(KV0 + 2 * t, w_in, c0, first=t == 0)
            with sp.Fori(1, HEADS + 1) as after:
                for t, c0 in enumerate((COL_K, COL_Q, COL_V, COL_QA, COL_Z)):
                    tile(HEAD0 - 10 + 10 * after + 2 * t, w_in, after * P + (c0 - P))
            with sp.Fori(0, KT) as m:
                tile(OUT0 + 2 * m, w_out, m * P)
            with sp.Fori(0, CHUNKS) as c:
                with sp.Fori(0, FC) as f:
                    for part in range(2):
                        tile(MLP0 + MLP_PER * c + 4 * f + 2 * part, w_up, part * DFF + (c * FC + f) * P)
                with sp.Fori(0, KT) as m:
                    u = MLP0 + MLP_PER * c + 4 * FC + 2 * m
                    for j, (k0, n_k) in enumerate(((0, 6), (6, FC - 6))):
                        load(j, u + j, w_down[bass.ds((c * FC + k0) * P, n_k * P), bass.ds(m * P, P)], n_k)
            for j in range(2):
                load(j, MLP0 + CHUNKS * MLP_PER + j, w_down[0:UK * P, 0:P], UK)
            for b in range(NB):
                sp.wait_ge(fin_taken.sem, 4 * (b + 1))
                sp.dma_start(out[0, b * P:(b + 1) * P, :], otok[:, b, :]).then_inc(stored, 16)
            sp.wait_ge(stored, 16 * NB)

        def group(t, h):
            return t[:].rearrange("p g n -> p (g n)")[:, bass.ds((h & 4) * (S // 4), S)]

        def at(t, i, width=S):
            return t[:, bass.ds(i * width, width)]

        @block.gpsimd
        def _(pool):
            for j in range(4):
                for k in range(KT):
                    n = j * KT + k
                    if n >= 4:
                        pool.wait_ge(ada_step.sem, n - 3)
                    pool.dma_start(ada_first[k % 4], A["w_ada"][0, k * P:(k + 1) * P, j * ADA_W:(j + 1) * ADA_W]) \
                        .then_inc(ada_in0[k % 4], 16)
            pool.wait_ge(*cols_made.after(0))
            nc.gpsimd.memset(pre[:, :, 0:1], 0.0).then_inc(pads_made.sem, 1)
            nc.gpsimd.memset(pre[:, :, S + 1:S + 2], 0.0).then_inc(pads_made.sem, 1)

            def ada_loads(h, g, first=False):
                for k in range(2 * g, 2 * g + 2):
                    if not (first and g == 0):
                        pool.wait_ge(ada_step.sem, (4 + h) * KT + k - 1)
                    pool.dma_start(ada_w[k % 2][:], A["w_ada"][0, k * P:(k + 1) * P, bass.ds((4 + h) * ADA_W, ADA_W)]) \
                        .then_inc(ada_in[k % 2], 16)

            def head(h, stream):
                if stream:
                    ada_loads(h + 1, 0)
                pool.wait_ge(*norm_made.after(h, 3))
                nc.gpsimd.tensor_copy(vcur.rearrange("p b n -> p (b n)"), group(va, h)).then_inc(vcur_made.sem, 1)
                if stream:
                    ada_loads(h + 1, 1)
                for n in range(LEVELS):
                    if n == 0:
                        pool.wait_ge(*ll_step.after(h))
                        pool.wait_ge(*av_sum.after(h))
                    elif n == 1:
                        pool.wait_ge(*t_first.after(h))
                        pool.wait_ge(*lt_sum.after(h))
                    else:
                        pool.wait_ge(*y_sum.after(h, n - 1))
                    mask = lvl[:, n].unsqueeze(2).broadcast_to([P, 2, NB, P])
                    nc.gpsimd.tensor_tensor(LM, LL[:], mask, ALU.mult).then_inc(lm_made.sem, 1)
                    if stream:
                        ada_loads(h + 1, 2 + n)

            for g in range(8):
                ada_loads(0, g, first=True)
            pool.wait_ge(*v_tok.after(1))
            head(0, True)
            with pool.Fori(1, HEADS - 1) as h:
                head(h, True)
            head(HEADS - 1, False)
            pool.wait_ge(*mx_lo.after(0))
            for b in range(NB):
                pool.dma_start(xtok[:, b, :], A["x"][0, b * P:(b + 1) * P, :]).then_inc(x2_loaded, 16)

        @block.scalar
        def _(act):
            for dst, src in ((rows[0:96, 0, :], A["b_ada"][0].rearrange("(n p) -> n p", p=P)),
                             (rows[96:97, 0, :], A["attn_q_norm"]),
                             (rows[97:98, 0, :], A["attn_k_norm"]),
                             (rows[98:99, 0, :], A["dn_norm_w"]),
                             (rows[99:115, 0, :], A["final_norm"].rearrange("(n p) -> n p", p=P)),
                             (rows[0:72, 1, :], A["dn_conv_w"][0].rearrange("t (n p) -> (t n) p", p=P)),
                             (rows[0:128, 2, :], A["w_ffn_conv"][0].rearrange("t (n p) -> (t n) p", p=P)[0:128]),
                             (rows[0:128, 3, :], A["w_ffn_conv"][0].rearrange("t (n p) -> (t n) p", p=P)[128:256]),
                             (rows[0:8, 4, :], A["w_ffn_conv"][0].rearrange("t (n p) -> (t n) p", p=P)[256:264]),
                             (rows[8:96, 4, :], A["b_ffn_conv"][0].rearrange("(n p) -> n p", p=P)),
                             (rows[0:16, 5, :], A["c"].rearrange("o (n p) -> (o n) p", p=P))):
                act.dma_start(dst, src).then_inc(rows_in, 16)
            act.dma_start(arow[:, 0:16], A["dn_dt_bias"].rearrange("o d h -> o (d h)")).then_inc(small_in, 16)
            act.dma_start(arow[:, 16:32], A["dn_A_log"].rearrange("o d h -> o (d h)")).then_inc(small_in, 16)
            for i in range(3):
                act.dma_start(lvl_f32[i], A["level_masks"][:, i * S:(i + 1) * S]).then_inc(lvl_in[i], 16)

            def split(q, slot, ahead=True):
                act.wait_ge(raw_in[slot], 16 * (q + 1))
                if ahead:
                    act.wait_ge(unit_used.sem, 2 * q + slot - 1)
                nc.scalar.activation(w_hi[slot][:], raw[slot][:], ACT.Copy).then_inc(hi_made.sem, 1)

            def s(h, j):
                split(HEAD0 // 2 + 5 * h + (j + 1) // 2, (j + 1) % 2)

            def evacuate(h, t, first=False):
                act.wait_ge(unit_used.sem, HEAD0 + 10 * h + 2 * t + 2)
                if t < 3:
                    if not first:
                        act.wait_ge(conv_step.sem, 9 * h - 9 + 3 * (t + 1))
                    dst = pre[:, t, 1:S + 1]
                else:
                    dst = at(mixedf, h if t == 3 else HEADS + h)
                nc.scalar.activation(dst, pw[t % 2][:], ACT.Copy).then_inc(tile_taken.sem, 1)

            act.wait_ge(*cols_made.after(0))
            nc.scalar.activation(cond[:], col[:, V_C:V_C + KT], ACT.Silu).then_inc(cond_made.sem, 1)
            act.wait_ge(*gate_row_sum.after(0))
            nc.scalar.activation(gates[:, 0, :], pd[2][:, 0:16], ACT.Copy).then_inc(gates_made.sem, 1)
            nc.scalar.activation(gates[:, 1, :], pd[2][:, 16:32], ACT.Exp).then_inc(gates_made.sem, 1)
            act.wait_ge(x_loaded, 16 * NB)
            for b in range(NB):
                if b:
                    act.wait_ge(*x_squared.after(0, b))
                nc.scalar.activation(junk, x_in[:, b, :], ACT.Square, accum_out=nrm[:, 0, b:b + 1]).then_inc(x_squared.sem, 1)
            act.wait_ge(*x_squared.after(0))
            nc.scalar.activation(nrm[:, 1, :], nrm[:, 0, :], ACT.Ln, scale=1.0 / DM, bias=eps1).then_inc(x_rstd.sem, 1)
            act.wait_ge(*x_rstd.after(0, 1))
            nc.scalar.activation(nrm[:, 2, :], nrm[:, 1, :], ACT.Exp, scale=-0.5).then_inc(x_rstd.sem, 1)
            split(0, 0, ahead=False)
            split(0, 1, ahead=False)
            for m in range(KT):
                act.wait_ge(*hn_full.after(0, m + 1))
                nc.scalar.activation(act_hi[:, m, :], hn_tmp[m % 2], ACT.Copy).then_inc(hn_hi.sem, 1)

            act.wait_ge(*ba_sum.after(0))
            nc.scalar.activation(gall[:, 0], pd[4][:, 0:128].rearrange("p (b n) -> p b n", n=32)[:, :, 0:16], ACT.Exp,
                                 scale=-1.0).then_inc(gate_a.sem, 1)
            act.wait_ge(*gate_v.after(0, 1))
            nc.scalar.activation(tmpf[:, 64:128], tmpf[:, 0:64], ACT.Abs).then_inc(gate_a.sem, 1)
            act.wait_ge(*gate_a.after(0, 2))
            nc.scalar.activation(tmpf[:, 64:128], tmpf[:, 64:128], ACT.Exp, scale=-1.0).then_inc(gate_a.sem, 1)
            act.wait_ge(*gate_a.after(0, 3))
            nc.scalar.activation(tmpf[:, 64:128], tmpf[:, 64:128], ACT.Ln, bias=1.0).then_inc(gate_a.sem, 1)
            act.wait_ge(*cum_sum.after(0))
            nc.scalar.activation(gall[:, 3], pd[3][:, 64:128], ACT.Exp).then_inc(gate_a.sem, 1)
            nc.scalar.activation(tmpf[:, 128:192], pd[3][:, 0:64], ACT.Exp).then_inc(gate_a.sem, 1)

            for t in range(4):
                split(t + 1, 0)
                act.wait_ge(unit_used.sem, 2 * t + 2)
                nc.scalar.activation(mixed[:, 12 + t, :], pw[t % 2][:], ACT.Copy).then_inc(tile_taken.sem, 1)
                split(t + 1, 1)
            act.wait_ge(*pads_made.after(0))
            for t in range(5):
                split(HEAD0 // 2 + t + 1, 0)
                evacuate(0, t, first=True)
                if t < 4:
                    split(HEAD0 // 2 + t + 1, 1)
            for g in range(KV_HEADS):
                act.wait_ge(tile_taken.sem, 4)
                if g:
                    act.wait_ge(kv_step.sem, 4 * g)
                nc.scalar.activation(sqa, mixed[:, 12 + g, :], ACT.Square).then_inc(kv_sq.sem, 1)
                act.wait_ge(*kv_ss.after(g))
                nc.scalar.activation(sqa, pd[2], ACT.Ln, scale=1.0 / P, bias=eps1).then_inc(kv_rstd.sem, 1)
                act.wait_ge(*kv_rstd.after(g, 1))
                nc.scalar.activation(sqa, sqa, ACT.Exp, scale=-0.5).then_inc(kv_rstd.sem, 1)
                act.wait_ge(*v_tr.after(g))
                nc.scalar.activation(va[:, g, :], pd[3], ACT.Copy).then_inc(v_tok.sem, 1)

            def head(h, stream, first=False):
                if stream:
                    s(h + 1, 0)
                if not first:
                    act.wait_ge(*mix_step.after(h - 1))
                act.wait_ge(tile_taken.sem, 4 + 5 * h + 5)
                for part, sq_to in ((0, tmp[:, 0, :]), (1, tmp[:, 1, :])):
                    act.wait_ge(*conv_step.after(h, 3 * (part + 1)))
                    nc.scalar.activation(act3[:, part, :], act3[:, part, :], ACT.Silu).then_inc(silu_done.sem, 1)
                    act.wait_ge(*silu_done.after(h, part + 1))
                    nc.scalar.activation(sq_to, act3[:, part, :], ACT.Square).then_inc(sq_done.sem, 1)
                nc.scalar.activation(sqa, at(mixedf, h), ACT.Square).then_inc(sq_done.sem, 1)
                act.wait_ge(*conv_step.after(h))
                nc.scalar.activation(act3[:, 2, :], act3[:, 2, :], ACT.Silu).then_inc(silu_done.sem, 1)
                nc.scalar.activation(at(mixedf, HEADS + h), at(mixedf, HEADS + h), ACT.Silu).then_inc(silu_done.sem, 1)
                act.wait_ge(*gc_sum.after(h))
                nc.scalar.activation(EGf, pd34, ACT.Exp).then_inc(eg_done.sem, 1)
                if stream:
                    s(h + 1, 1)
                for i, (to, scale, eps) in enumerate(((tmp[:, 0, :], 1.0, eps1), (tmp[:, 1, :], float(P), eps128),
                                                      (sqa, 1.0 / P, eps1))):
                    act.wait_ge(*ss_sum.after(h, i + 1))
                    nc.scalar.activation(to, pd[i], ACT.Ln, scale=scale, bias=eps).then_inc(ln_done.sem, 1)
                for i, to in enumerate((tmp[:, 0, :], tmp[:, 1, :], sqa)):
                    act.wait_ge(*ln_done.after(h, i + 1))
                    nc.scalar.activation(to, to, ACT.Exp, scale=-0.5).then_inc(rstd_made.sem, 1)
                if stream:
                    evacuate(h + 1, 0)
                    s(h + 1, 2)
                act.wait_ge(*ll_masked.after(h))
                nc.scalar.activation(LLf, LLf, ACT.Exp, scale=-1.0).then_inc(decay_done.sem, 1)
                nc.scalar.activation(DQf, DQf, ACT.Exp).then_inc(decay_done.sem, 1)
                for i, (to, bank) in enumerate(((ktf, pd[3]), (vtf, pd[4]))):
                    act.wait_ge(*tr_sum.after(h, i + 1))
                    nc.scalar.activation(to, bank, ACT.Copy).then_inc(tok_done.sem, 1)

                def weigh(b):
                    act.wait_ge(soft_step.sem, 4 * NB * h + SOFT_MAX[b])
                    nc.scalar.activation(prob[b % 2], pd[2 - b % 2], ACT.Exp, scale=SCALE, bias=soft[:, 1, b:b + 1],
                                         accum_out=soft[:, 2, b:b + 1]).then_inc(p_exp.sem, 1)

                def turned(b):
                    act.wait_ge(*pt_sum.after(h, b + 1))
                    nc.scalar.activation(PT[:, :, b * P:(b + 1) * P], pd[3 + b % 2].rearrange("p (k q) -> p k q", q=P),
                                         ACT.Copy).then_inc(pt_taken.sem, 1)

                weigh(0)
                weigh(1)
                if stream:
                    s(h + 1, 3)
                turned(0)
                act.wait_ge(*pt_sum.after(h, 1))
                weigh(2)
                turned(1)
                weigh(3)
                turned(2)
                turned(3)
                if stream:
                    evacuate(h + 1, 1)
                if stream:
                    s(h + 1, 4)
                for n in range(1, LEVELS):
                    act.wait_ge(*y_sum.after(h, n))
                    nc.scalar.activation(Yf, pd01, ACT.Copy).then_inc(y_taken.sem, 1)
                    if stream:
                        s(h + 1, 4 + n)
                        if n in (2, 4):
                            evacuate(h + 1, 2 + (n == 4))
                act.wait_ge(*u_sum.after(h))
                nc.scalar.activation(LLf, pd01, ACT.Copy).then_inc(u_taken.sem, 1)
                if stream:
                    evacuate(h + 1, 4)
                act.wait_ge(*o_sum.after(h, 1))
                nc.scalar.activation(act3[:, 1, :], pd[4], ACT.Copy).then_inc(o_taken.sem, 1)
                act.wait_ge(*o_summed.after(h))
                nc.scalar.activation(tmp[:, 0, :], act3[:, 1, :], ACT.Square).then_inc(onorm.sem, 1)
                act.wait_ge(*sso_sum.after(h))
                nc.scalar.activation(tmp[:, 1, :], pd[2], ACT.Ln, scale=1.0 / P, bias=eps1).then_inc(onorm.sem, 1)
                act.wait_ge(*onorm.after(h, 2))
                nc.scalar.activation(tmp[:, 1, :], tmp[:, 1, :], ACT.Exp, scale=-0.5).then_inc(onorm.sem, 1)

            head(0, True, first=True)
            with act.Fori(1, HEADS - 1) as h:
                head(h, True)
            head(HEADS - 1, False)

            act.wait_ge(*av_taken.after(HEADS - 1))
            act.wait_ge(*mix_step.after(HEADS - 1))
            act.wait_ge(unit_used.sem, OUT0)
            for m in range(KT):
                nc.scalar.activation(act_hi[:, m, :], mixed[:, m, :], ACT.Copy).then_inc(mx_hi.sem, 1)
            split(OUT0 // 2, 1)
            for m in range(2):
                split(OUT0 // 2 + m + 1, 0)
                if m == 0:
                    split(OUT0 // 2 + 1, 1)
            for m in range(KT):
                act.wait_ge(*x2_sum.after(0, m + 1))
                nc.scalar.activation(hT[:, m, :], pd[m % 6], ACT.Copy).then_inc(x2_taken.sem, 1)

            def square(m):
                act.wait_ge(out_taken.sem, m + 1)
                act.wait_ge(sqacc_step.sem, 1 + m)
                nc.scalar.activation(sq[:], at(hTf, m), ACT.Square).then_inc(sq_made.sem, 1)

            split(OUT0 // 2 + 2, 1)
            square(0)
            square(1)
            with act.Fori(2, KT) as m:
                split(OUT0 // 2 + m + 1, 0)
                split(OUT0 // 2 + m + 1, 1)
                square(m)

            def inverse_rms(i):
                act.wait_ge(*ssum.after(i))
                nc.scalar.activation(rstd[:], pd[0], ACT.Ln, scale=1.0 / DM, bias=eps1).then_inc(rstd_step.sem, 1)
                act.wait_ge(*rstd_step.after(i, 1))
                nc.scalar.activation(rstd[:], rstd[:], ACT.Exp, scale=-0.5).then_inc(rstd_step.sem, 1)

            inverse_rms(0)
            act.wait_ge(out_taken.sem, KT)
            nc.scalar.activation(gp[:, :, 0:1], cst[:, C_ZERO:C_ZERO + 2].unsqueeze(2), ACT.Copy).then_inc(up_taken.sem, 1)
            nc.scalar.activation(gp[:, :, S + 1:S + 2], cst[:, C_ZERO:C_ZERO + 2].unsqueeze(2), ACT.Copy).then_inc(up_taken.sem, 1)
            for m in range(KT):
                act.wait_ge(*h2_step.after(0, 2 * m + 2))
                nc.scalar.activation(act_hi[:, m, :], hn2[:, m % 2, :], ACT.Copy).then_inc(h2_hi.sem, 1)

            with act.Fori(0, CHUNKS) as c:
                base = MLP0 // 2 + MLP_PER // 2 * c
                with act.Fori(0, FC) as f:
                    n = FC * c + f
                    pair = base + 2 * f

                    def up(part):
                        act.wait_ge(unit_used.sem, 2 * pair + 2 * part + 2)
                        act.wait_ge(fconv_step.sem, 6 * n + 3 * part + 3)
                        nc.scalar.activation(gp[:, part, 1:S + 1], pw[part][:], ACT.Copy).then_inc(up_taken.sem, 1)

                    split(pair + 1, 0)
                    up(0)
                    split(pair + 1, 1)
                    act.wait_ge(fconv_step.sem, 6 * n + 9)
                    nc.scalar.activation(cv[:, 0, :], cv[:, 0, :], ACT.Silu).then_inc(fsilu.sem, 1)
                    split(pair + 2, 0)
                    up(1)
                    split(pair + 2, 1)
                    act.wait_ge(*fprod.after(n))
                    act.wait_ge(unit_used.sem, 2 * base)
                    nc.scalar.activation(at(mhf_hi, f), prod[:], ACT.Copy).then_inc(mh_hi_made.sem, 1)
                with act.Fori(0, KT) as m:
                    split(base + 2 * FC + m + 1, 0)
                    split(base + 2 * FC + m + 1, 1)
            for m in range(KT):
                act.wait_ge(out_taken.sem, KT * (CHUNKS + 1))
                act.wait_ge(sqacc_step.sem, KT + 1 + m)
                nc.scalar.activation(sq[:], hT[:, m, :], ACT.Square).then_inc(sq_made.sem, 1)
            inverse_rms(1)
            for i in range(KT):
                b, g = i // 4, i % 4
                act.wait_ge(*fin_sum.after(0, i + 1))
                nc.scalar.activation(otok[:, b, g * S:(g + 1) * S], pd[i % 6], ACT.Copy).then_inc(fin_taken.sem, 1)

        @block.vector
        def _(dve):
            V = nc.vector

            def low(q, slot):
                dve.wait_ge(hi_made.sem, 2 * q + slot + 1)
                V.tensor_tensor(w_lo[slot][:], raw[slot][:], w_hi[slot][:].bitcast(F32), ALU.subtract).then_inc(lo_made.sem, 1)

            def s(h, j):
                low(HEAD0 // 2 + 5 * h + (j + 1) // 2, (j + 1) % 2)

            def ada_add(w, in_sem, in_val, j, k, first=False):
                dve.wait_ge(in_sem, in_val)
                if k == 0:
                    if not first:
                        dve.wait_ge(*ada_sum.after(j - 1))
                    V.tensor_scalar(ada_acc[:], w, cond[:, k:k + 1], None, ALU.mult).then_inc(ada_step.sem, 1)
                else:
                    dve.wait_ge(ada_step.sem, KT * j + k)
                    V.scalar_tensor_tensor(ada_acc[:], w, cond[:, k:k + 1], ada_acc[:], ALU.mult, ALU.add) \
                        .then_inc(ada_step.sem, 1)

            def ada_group(h, g):
                for k in (2 * g, 2 * g + 1):
                    ada_add(ada_w[k % 2][:], ada_in[k % 2], 16 * (8 * h + k // 2 + 1), 4 + h, k)

            def ada_columns(j):
                dve.wait_ge(*ada_sum.after(j))
                V.tensor_tensor(at(mod, j, 8), pd[5][:, 0:8], at(col, j, 8), ALU.add).then_inc(ada_out.sem, 1)

            dve.wait_ge(*cols_sum.after(0))
            V.tensor_copy(col[:, 0:443], pd[0][:, 0:443]).then_inc(cols_made.sem, 1)
            V.tensor_copy(col[:, 443:V_N], pd[1][:, 0:V_N - 443]).then_inc(cols_made.sem, 1)
            for i in range(3):
                dve.wait_ge(lvl_in[i], 16)
                V.tensor_copy(lvl[:, 2 * i:2 * i + 2], lvl_f32[i].rearrange("p (l d n) -> p l d n", l=2, d=2)) \
                    .then_inc(lvl_made.sem, 1)
            dve.wait_ge(*cond_made.after(0))
            for j in range(4):
                for k in range(KT):
                    ada_add(ada_first[k % 4], ada_in0[k % 4], 16 * (4 * j + k // 4 + 1), j, k, first=j == 0)
                if j == 0:
                    for b in range(NB):
                        dve.wait_ge(*x_rstd.after(0))
                        V.tensor_scalar(x_in[:, b, :], x_in[:, b, :], nrm[:, 2, b:b + 1], None, ALU.mult) \
                            .then_inc(x_normed.sem, 1)
                ada_columns(j)
            dve.wait_ge(ada_out.sem, 4)
            V.tensor_scalar(mod[:, 16:32], mod[:, 16:32], 1.0, None, ALU.add).then_inc(scale_made.sem, 1)
            low(0, 0)
            low(0, 1)
            dve.wait_ge(*scale_made.after(0))

            def hn_low(m):
                dve.wait_ge(*hn_hi.after(0, m + 1))
                V.tensor_tensor(act_lo[:, m, :], hn_tmp[m % 2], act_hi[:, m, :].bitcast(F32), ALU.subtract) \
                    .then_inc(hn_lo.sem, 1)

            for m in range(KT):
                dve.wait_ge(*xt_sum.after(0, m + 1))
                if m >= 2:
                    dve.wait_ge(*hn_lo.after(0, m - 1))
                V.tensor_scalar(hn_tmp[m % 2], pd[m % 4], mod[:, 16 + m:17 + m], mod[:, m:m + 1], ALU.mult, ALU.add) \
                    .then_inc(hn_full.sem, 1)
                if m:
                    hn_low(m - 1)
            hn_low(KT - 1)

            dve.wait_ge(*gates_made.after(0))
            dve.wait_ge(*gate_a.after(0, 1))
            dve.wait_ge(*hn_lo.after(0))
            four = lambda t: t.rearrange("p (b n) -> p b n", n=16)
            t_x, t_s = four(tmpf[:, 0:64]), four(tmpf[:, 64:128])
            g_all = gall[:, 1].rearrange("p b d h -> p b (d h)")
            V.tensor_tensor(t_x, pd[4][:, 0:128].rearrange("p (b n) -> p b n", n=32)[:, :, 16:32],
                            gates[:, 0, :].unsqueeze(1).broadcast_to([P, NB, 16]), ALU.add).then_inc(gate_v.sem, 1)
            V.tensor_scalar(gall[:, 0], gall[:, 0], 1.0, None, ALU.add).then_inc(gate_v.sem, 1)
            dve.wait_ge(*gate_v.after(0, 2))
            V.reciprocal(gall[:, 0], gall[:, 0]).then_inc(gate_v.sem, 1)
            dve.wait_ge(*gate_a.after(0, 4))
            V.scalar_tensor_tensor(g_all, t_x, 0.0, t_s, ALU.max, ALU.add).then_inc(gate_v.sem, 1)
            dve.wait_ge(*gate_v.after(0, 4))
            V.scalar_tensor_tensor(g_all, g_all, -1.0, gates[:, 1, :].unsqueeze(1).broadcast_to([P, NB, 16]),
                                   ALU.mult, ALU.mult).then_inc(gate_v.sem, 1)
            dve.wait_ge(*gate_a.after(0))
            V.tensor_copy(gall[:, 2], pd[3][:, 0:64]).then_inc(gate_v.sem, 1)
            V.tensor_tensor(gall[:, 4], gall[:, 0], tmpf[:, 128:192], ALU.mult).then_inc(gate_v.sem, 1)

            for t in range(4):
                low(t + 1, 0)
                low(t + 1, 1)
            for t in range(5):
                low(HEAD0 // 2 + t + 1, 0)
                if t < 4:
                    low(HEAD0 // 2 + t + 1, 1)
            for g in range(KV_HEADS):
                dve.wait_ge(*kv_rstd.after(g))
                V.scalar_tensor_tensor(ka[:, g, :], mixed[:, 12 + g, :], col[:, V_KN:V_KN + 1], sqa, ALU.mult, ALU.mult) \
                    .then_inc(kv_step.sem, 1)
                dve.wait_ge(*kv_rot.after(g))
                V.tensor_tensor(rotsin, pd[1], sinT, ALU.mult).then_inc(kv_step.sem, 1)
                V.tensor_tensor(ka[:, g, :], ka[:, g, :], cosT, ALU.mult).then_inc(kv_step.sem, 1)
                dve.wait_ge(*kv_step.after(g, 3))
                V.tensor_tensor(ka[:, g, :], ka[:, g, :], rotsin, ALU.add).then_inc(kv_step.sem, 1)
            for g in range(8):
                ada_group(0, g)
            dve.wait_ge(*pads_made.after(0))
            dve.wait_ge(*lvl_made.after(0))

            def head(h, stream):
                ada_columns(4 + h)
                V.tensor_copy(gcur[:].rearrange("p a b d -> p (a b d)"),
                              gall[:].rearrange("p a b d h -> p (a b d) h")[:, :, bass.ds(h, 1)].squeeze(2)) \
                    .then_inc(gcur_made.sem, 1)
                dve.wait_ge(*gcur_made.after(h))
                for d in range(2):
                    V.tensor_tensor(LL[:, d], cst[:, C_CUM + d * P:C_CUM + (d + 1) * P].unsqueeze(1).broadcast_to([P, NB, P]),
                                    gcur[:, 1, :, d].unsqueeze(2).broadcast_to([P, NB, P]), ALU.mult).then_inc(gu_made.sem, 1)
                for part, tile in enumerate((8, 0, 16)):
                    dve.wait_ge(tile_taken.sem, 4 + 5 * h + part + 1)
                    w = [col[:, bass.ds(V_CONV + 24 * j + tile + h, 1)] for j in range(TAPS)]
                    V.tensor_scalar(act3[:, part, :], pre[:, part, 0:S], w[0], None, ALU.mult).then_inc(conv_step.sem, 1)
                    for j in (1, 2):
                        dve.wait_ge(*conv_step.after(h, 3 * part + j))
                        V.scalar_tensor_tensor(act3[:, part, :], pre[:, part, j:j + S], w[j], act3[:, part, :],
                                               ALU.mult, ALU.add).then_inc(conv_step.sem, 1)
                if stream:
                    s(h + 1, 0)
                dve.wait_ge(*gc_sum.after(h))
                dve.wait_ge(*eg_done.after(h))
                for d in range(2):
                    V.tensor_tensor(LL[:, d], pd[3 + d].rearrange("p (b n) -> p b n", n=P),
                                    gcur[:, 2, :, d].unsqueeze(2).broadcast_to([P, NB, P]), ALU.subtract) \
                        .then_inc(diff_made.sem, 1)
                dve.wait_ge(*diff_made.after(h))
                masks = [cst[:, c:c + 2 * P].rearrange("p (d n) -> p d n", n=P).unsqueeze(2).broadcast_to([P, 2, NB, P])
                         for c in (C_MQ, C_ML)]
                V.tensor_tensor(DQ[:], LL[:], masks[0], ALU.subtract).then_inc(dq_masked.sem, 1)
                V.tensor_tensor(LL[:], LL[:], masks[1], ALU.add).then_inc(ll_masked.sem, 1)
                for i in range(2):
                    dve.wait_ge(*rstd_made.after(h, i + 1))
                    V.tensor_tensor(act3[:, i, :], act3[:, i, :], tmp[:, i, :], ALU.mult).then_inc(norm_made.sem, 1)
                dve.wait_ge(*rstd_made.after(h))
                V.scalar_tensor_tensor(qr, at(mixedf, h), col[:, V_QN:V_QN + 1], sqa, ALU.mult, ALU.mult) \
                    .then_inc(norm_made.sem, 1)
                if stream:
                    s(h + 1, 1)
                dve.wait_ge(*rot_sum.after(h))
                V.tensor_tensor(rotsin, pd[1], sinT, ALU.mult).then_inc(rot_scaled.sem, 1)
                V.tensor_tensor(qr, qr, cosT, ALU.mult).then_inc(rope_step.sem, 1)
                dve.wait_ge(*rot_scaled.after(h))
                dve.wait_ge(*rope_step.after(h, 1))
                V.tensor_tensor(qr, qr, rotsin, ALU.add).then_inc(rope_step.sem, 1)
                if stream:
                    s(h + 1, 2)
                both = lambda t: t.unsqueeze(1).broadcast_to([P, 2, S])
                side = lambda t: t.rearrange("p (d n) -> p d n", n=S)
                factor = lambda i: gcur[:, i].rearrange("p b d -> p d b").unsqueeze(3).broadcast_to([P, 2, NB, P])
                dve.wait_ge(*decay_done.after(h, 1))
                dve.wait_ge(*g_sum.after(h))
                V.tensor_tensor(side(LLf), both(pd[5]), side(LLf), ALU.mult).then_inc(ll_step.sem, 1)
                dve.wait_ge(*ll_step.after(h, 1))
                V.tensor_tensor(LL[:], LL[:], factor(0), ALU.mult).then_inc(ll_step.sem, 1)
                dve.wait_ge(*decay_done.after(h))
                dve.wait_ge(*qk_sum.after(h))
                V.tensor_tensor(side(DQf), both(pd[0]), side(DQf), ALU.mult).then_inc(qk_made.sem, 1)
                if stream:
                    ada_group(h + 1, 0)

                def score_max(b):
                    dve.wait_ge(*sc_sum.after(h, b + 1))
                    n = SOFT_MAX[b] - 2
                    V.tensor_reduce(soft[:, 0, b:b + 1], pd[2 - b % 2], AX.X, ALU.max).then_inc(soft_step.sem, 1)
                    dve.wait_ge(soft_step.sem, 16 * h + n + 1)
                    V.tensor_scalar(soft[:, 1, b:b + 1], soft[:, 0, b:b + 1], -SCALE, None, ALU.mult).then_inc(soft_step.sem, 1)

                def score_norm(b):
                    dve.wait_ge(*p_exp.after(h, b + 1))
                    n = SOFT_OUT[b] - 2
                    V.reciprocal(soft[:, 3, b:b + 1], soft[:, 2, b:b + 1]).then_inc(soft_step.sem, 1)
                    dve.wait_ge(soft_step.sem, 16 * h + n + 1)
                    V.tensor_scalar(prob[b % 2], prob[b % 2], soft[:, 3, b:b + 1], None, ALU.mult).then_inc(soft_step.sem, 1)

                score_max(0)
                score_max(1)
                score_norm(0)
                score_max(2)
                score_norm(1)
                if stream:
                    s(h + 1, 3)
                score_max(3)
                score_norm(2)
                score_norm(3)
                if stream:
                    ada_group(h + 1, 1)
                dve.wait_ge(*tok_done.after(h, 1))
                V.tensor_tensor(tmpf.rearrange("p (d b n) -> p d b n", d=2, b=NB),
                                ktok[:].unsqueeze(1).broadcast_to([P, 2, NB, P]), factor(3), ALU.mult).then_inc(kd_made.sem, 1)
                V.tensor_copy(glast[:, 0, :], EG[:, 0, :].rearrange("p (c n) -> p c n", n=DN)[:, :, DN - 1]).then_inc(gl_made.sem, 1)
                V.tensor_copy(glast[:, 1, :], EG[:, 1, :].rearrange("p (c n) -> p c n", n=DN)[:, :, 0]).then_inc(gl_made.sem, 1)
                dve.wait_ge(*gl_made.after(h))
                V.tensor_tensor(EG[:], EG[:], both(act3[:, 1, :]), ALU.mult).then_inc(qd_made.sem, 1)
                dve.wait_ge(*av_sum.after(h))
                V.tensor_scalar(at(mixedf, h), pd[2], 1.0, None, ALU.mult).then_inc(av_taken.sem, 1)
                if stream:
                    s(h + 1, 4)
                eye = ident.unsqueeze(1).broadcast_to([P, 2 * NB, P])
                eight = lambda t: t.rearrange("p (a n) -> p a n", n=P)
                dve.wait_ge(*lm_made.after(h, 1))
                V.tensor_tensor(eight(Tf), eye, eight(LMf), ALU.subtract).then_inc(t_first.sem, 1)
                dve.wait_ge(*lt_sum.after(h))
                V.tensor_tensor(eight(TTf), eye, eight(pd01), ALU.subtract).then_inc(t_first.sem, 1)
                if stream:
                    ada_group(h + 1, 2)
                for n in range(1, LEVELS):
                    if n < LEVELS - 1:
                        dve.wait_ge(*a_sum.after(h, 2 * n))
                        V.tensor_tensor(Tf, Tf, pd23, ALU.subtract).then_inc(t_step.sem, 1)
                    dve.wait_ge(*a_sum.after(h, min(2 * n, 9)))
                    V.tensor_tensor(TTf, TTf, pd45, ALU.subtract).then_inc(t_step.sem, 1)
                    if stream:
                        s(h + 1, 4 + n)
                        ada_group(h + 1, 2 + n)
                dve.wait_ge(*t_step.after(h))
                V.tensor_tensor(T[:], TT[:], factor(0), ALU.mult).then_inc(tb_made.sem, 1)
                V.tensor_tensor(TT[:], TT[:], factor(4), ALU.mult).then_inc(tb_made.sem, 1)
                dve.wait_ge(*wt_sum.after(h))
                V.tensor_copy(Yf, pd23).then_inc(wt_taken.sem, 1)
                dve.wait_ge(*u_taken.after(h))
                for c in range(NCH):
                    for d in range(2):
                        if c:
                            n = 2 * (c - 1) + d
                            cc = c if d == 0 else NCH - 1 - c
                            r = slice(DN * (cc % 2), DN * (cc % 2) + DN)
                            dve.wait_ge(*vn_sum.after(h, n + 1))
                            V.tensor_tensor(vn[r, d, :], LL[r, d, cc // 2, :], pd[d][r, 0:P], ALU.subtract) \
                                .then_inc(vnew_made.sem, 1)
                    for d in range(2):
                        if c < NCH - 1:
                            cc = c if d == 0 else NCH - 1 - c
                            dve.wait_ge(*s_sum.after(h, 2 * c + d + 1))
                            if c == 0:
                                V.tensor_copy(st[:, d, :], pd[d][:, P:2 * P]).then_inc(state_made.sem, 1)
                            else:
                                dve.wait_ge(*state_made.after(h, 2 * (c - 1) + d + 1))
                                V.scalar_tensor_tensor(st[:, d, :], st[:, d, :], glast[:, d, cc:cc + 1], pd[d][:, P:2 * P],
                                                       ALU.mult, ALU.add).then_inc(state_made.sem, 1)
                dve.wait_ge(*o_sum.after(h))
                dve.wait_ge(*o_taken.after(h))
                V.tensor_tensor(act3[:, 1, :], act3[:, 1, :], pd[5], ALU.add).then_inc(o_summed.sem, 1)
                dve.wait_ge(*onorm.after(h))
                V.scalar_tensor_tensor(act3[:, 1, :], act3[:, 1, :], col[:, V_DNW:V_DNW + 1], tmp[:, 1, :],
                                       ALU.mult, ALU.mult).then_inc(mix_step.sem, 1)
                dve.wait_ge(*mix_step.after(h, 1))
                V.tensor_tensor(at(mixedf, HEADS + h), act3[:, 1, :], at(mixedf, HEADS + h), ALU.mult).then_inc(mix_step.sem, 1)

            head(0, True)
            with dve.Fori(1, HEADS - 1) as h:
                head(h, True)
            head(HEADS - 1, False)

            for m in range(KT):
                dve.wait_ge(*mx_hi.after(0, m + 1))
                V.tensor_tensor(act_lo[:, m, :], mixed[:, m, :], act_hi[:, m, :].bitcast(F32), ALU.subtract) \
                    .then_inc(mx_lo.sem, 1)
            dve.wait_ge(ada_out.sem, ADA_STEPS)
            V.tensor_scalar(mod[:, 64:80], mod[:, 64:80], 1.0, None, ALU.add).then_inc(scale2_made.sem, 1)
            low(OUT0 // 2, 1)
            for m in range(2):
                low(OUT0 // 2 + m + 1, 0)
                if m == 0:
                    low(OUT0 // 2 + 1, 1)
            dve.wait_ge(*mx_lo.after(0))
            V.memset(sqacc[:], 0.0).then_inc(sqacc_step.sem, 1)

            def residual(unit_end, m, n, gate):
                dve.wait_ge(unit_used.sem, unit_end)
                V.scalar_tensor_tensor(at(hTf, m), bank_of(n), mod[:, bass.ds(gate + m, 1)], at(hTf, m), ALU.mult, ALU.add) \
                    .then_inc(out_taken.sem, 1)

            def add_square(m):
                dve.wait_ge(sq_made.sem, m + 1)
                dve.wait_ge(sqacc_step.sem, 1 + m)
                V.tensor_tensor(sqacc[:], sqacc[:], sq[:], ALU.add).then_inc(sqacc_step.sem, 1)

            dve.wait_ge(*x2_taken.after(0))
            for m in range(2):
                bank_of = lambda n: pw[n % 2][:]
                residual(OUT0 + 2 * m + 2, m, m, 32)
            low(OUT0 // 2 + 2, 1)
            add_square(0)
            add_square(1)
            with dve.Fori(1, KT // 2) as i:
                for j in range(2):
                    m = 2 * i + j
                    low(OUT0 // 2 + m + 1, 0)
                    low(OUT0 // 2 + m + 1, 1)
                    bank_of = lambda n, j=j: pw[j][:]
                    residual(OUT0 + 2 * m + 2, m, m, 32)
                    add_square(m)
            dve.wait_ge(*rstd_step.after(0))
            dve.wait_ge(*scale2_made.after(0))

            def h2_low(m):
                dve.wait_ge(*h2_hi.after(0, m + 1))
                V.tensor_tensor(act_lo[:, m, :], hn2[:, m % 2, :], act_hi[:, m, :].bitcast(F32), ALU.subtract) \
                    .then_inc(h2_lo.sem, 1)

            for m in range(KT):
                if m >= 2:
                    dve.wait_ge(*h2_lo.after(0, m - 1))
                V.tensor_tensor(hn2[:, m % 2, :], hT[:, m, :], rstd[:], ALU.mult).then_inc(h2_step.sem, 1)
                dve.wait_ge(*h2_step.after(0, 2 * m + 1))
                V.tensor_scalar(hn2[:, m % 2, :], hn2[:, m % 2, :], mod[:, 64 + m:65 + m], mod[:, 48 + m:49 + m],
                                ALU.mult, ALU.add).then_inc(h2_step.sem, 1)
                if m:
                    h2_low(m - 1)
            h2_low(KT - 1)
            V.memset(cv[:, 0, 0:1], 0.0).then_inc(fconv_step.sem, 3)
            V.memset(cv[:, 1, 0:1], 0.0).then_inc(fconv_step.sem, 3)

            with dve.Fori(0, CHUNKS) as c:
                base = MLP0 // 2 + MLP_PER // 2 * c
                with dve.Fori(0, FC) as f:
                    n = FC * c + f
                    pair = base + 2 * f

                    def convolve(part):
                        w = [col[:, bass.ds(V_FCONV + 2 * FT * j + part * FT + n, 1)] for j in range(TAPS)]
                        bias = col[:, bass.ds(V_FB + part * FT + n, 1)]
                        dve.wait_ge(up_taken.sem, 2 * n + part + 3)
                        V.tensor_scalar(cv[:, part, :], gp[:, part, 0:S], w[0], bias, ALU.mult, ALU.add) \
                            .then_inc(fconv_step.sem, 1)
                        for j in (1, 2):
                            dve.wait_ge(fconv_step.sem, 6 * n + 6 + 3 * part + j)
                            V.scalar_tensor_tensor(cv[:, part, :], gp[:, part, j:j + S], w[j], cv[:, part, :], ALU.mult, ALU.add) \
                                .then_inc(fconv_step.sem, 1)

                    low(pair + 1, 0)
                    convolve(0)
                    low(pair + 1, 1)
                    low(pair + 2, 0)
                    convolve(1)
                    low(pair + 2, 1)
                    dve.wait_ge(*fsilu.after(n))
                    dve.wait_ge(*fconv_step.after(n + 1))
                    V.tensor_tensor(prod[:], cv[:, 0, :], cv[:, 1, :], ALU.mult).then_inc(fprod.sem, 1)
                    dve.wait_ge(*mh_hi_made.after(n))
                    V.tensor_tensor(at(mhf_lo, f), prod[:], at(mhf_hi, f).bitcast(F32), ALU.subtract) \
                        .then_inc(mh_lo_made.sem, 1)
                with dve.Fori(0, KT // 2) as i:
                    for j in range(2):
                        m = 2 * i + j
                        low(base + 2 * FC + m + 1, 0)
                        low(base + 2 * FC + m + 1, 1)
                        bank_of = lambda n, j=j: pw[j][:]
                        residual(2 * base + 4 * FC + 2 * m + 2, m, m, 80)
            for m in range(KT):
                dve.wait_ge(sq_made.sem, KT + m + 1)
                if m:
                    dve.wait_ge(sqacc_step.sem, KT + 1 + m)
                    V.tensor_tensor(sqacc[:], sqacc[:], sq[:], ALU.add).then_inc(sqacc_step.sem, 1)
                else:
                    V.tensor_copy(sqacc[:], sq[:]).then_inc(sqacc_step.sem, 1)
            dve.wait_ge(*rstd_step.after(1))
            for m in range(KT):
                V.scalar_tensor_tensor(hT[:, m, :], hT[:, m, :], col[:, V_FN + m:V_FN + m + 1], rstd[:], ALU.mult, ALU.mult) \
                    .then_inc(fin_made.sem, 1)

        @block.tensor
        def _(pe):
            M, TR = pe.matmul, pe.transpose

            def part(q, slot, half, bank, free=None, start=None, stop=None, n_k=UK, k0=None, hi=act_hi, lo=act_lo):
                k0 = slot * UK if k0 is None else k0
                ks = range(n_k) if half is None else range(half * n_k // 2, (half + 1) * n_k // 2)
                if ks[0] == 0:
                    pe.wait_ge(lo_made.sem, 2 * q + slot + 1)
                for k in ks:
                    first, last = slot == 0 and k == 0, slot == 1 and k == n_k - 1
                    M(bank, w_hi[slot][:, k, :], hi[:, k0 + k, :], start=first, stop=False)
                    M(bank, w_hi[slot][:, k, :], lo[:, k0 + k, :], start=False, stop=False)
                    ins = M(bank, w_lo[slot][:, k, :], hi[:, k0 + k, :], start=False, stop=last)
                if ks[-1] == n_k - 1:
                    ins.then_inc(unit_used.sem, 1)

            def stream(h, j, half):
                t = j // 2
                if j % 2 == 0 and half == 0:
                    pe.wait_ge(tile_taken.sem, 4 + 5 * h + t - (1 if t else 0))
                part(HEAD0 // 2 + 5 * h + t, j % 2, half, pw[t % 2][:])

            def whole(q, bank, n_k=(UK, UK), hi=act_hi, lo=act_lo):
                part(q, 0, None, bank, n_k=n_k[0], k0=0, hi=hi, lo=lo)
                part(q, 1, None, bank, n_k=n_k[1], k0=n_k[0], hi=hi, lo=lo)

            pe.wait_ge(consts_in, 16)
            pe.wait_ge(rows_in, 16 * 11)
            at_col = 0
            for i, n in enumerate((115, 72, 128, 128, 96, 16)):
                bank, c0 = (0, at_col) if i < 4 else (1, at_col - 443)
                ins = TR(pd[bank][:, c0:c0 + n], rows[0:n, i, :], ident[0:n, 0:n])
                at_col += n
            ins.then_inc(cols_sum.sem, 1)
            pe.wait_ge(small_in, 32)
            M(pd[2][:, 0:32], ones[0:1, :], arow, start=True, stop=True).then_inc(gate_row_sum.sem, 1)

            def ada_sums(j):
                pe.wait_ge(*ada_step.after(j))
                for i in range(8):
                    ins = M(pd[5][:, i:i + 1], ada_acc[:, i * P:(i + 1) * P], ones[:, 0:1], start=True, stop=True)
                ins.then_inc(ada_sum.sem, 1)

            for j in range(4):
                if j:
                    pe.wait_ge(*ada_out.after(j - 1))
                ada_sums(j)
            pe.wait_ge(*x_normed.after(0))
            pe.wait_ge(*gates_made.after(0))
            for m in range(KT):
                if m >= 4:
                    pe.wait_ge(*hn_full.after(0, m - 3))
                for b in range(NB):
                    ins = TR(pd[m % 4][:, b * P:(b + 1) * P], x_in[:, b, m * P:(m + 1) * P], ident)
                ins.then_inc(xt_sum.sem, 1)
            pe.wait_ge(ba_in, 16)
            pe.wait_ge(*hn_lo.after(0))
            for b in range(NB):
                for k in range(KT):
                    for i, t in enumerate((act_hi, act_lo)):
                        ins = M(pd[4][:, b * 32:(b + 1) * 32], t[:, k, b * P:(b + 1) * P].bitcast(F32), wba[:, k, :],
                                start=k == 0 and i == 0, stop=k == KT - 1 and i == 1)
            ins.then_inc(ba_sum.sem, 1)
            pe.wait_ge(*gate_v.after(0, 5))
            for i, c0 in enumerate((C_CUM, C_REST)):
                for b in range(NB):
                    for d in range(2):
                        o = i * 64 + b * 16 + d * 8
                        ins = M(pd[3][:, o:o + 8], cst[:, c0 + d * P:c0 + (d + 1) * P], gall[:, 1, b, d, :], start=True, stop=True)
            ins.then_inc(cum_sum.sem, 1)
            for t in range(4):
                if t >= 2:
                    pe.wait_ge(tile_taken.sem, t - 1)
                whole(t, pw[t % 2][:])
            for j in range(10):
                stream(0, j, 0)
                stream(0, j, 1)
            for g in range(KV_HEADS):
                pe.wait_ge(*kv_sq.after(g))
                M(pd[2], ones, sqa, start=True, stop=True).then_inc(kv_ss.sem, 1)
                pe.wait_ge(kv_step.sem, 4 * g + 1)
                M(pd[1], rot, ka[:, g, :], start=True, stop=True).then_inc(kv_rot.sem, 1)
                if g:
                    pe.wait_ge(*v_tok.after(g - 1))
                for b in range(NB):
                    ins = TR(pd[3][:, b * P:(b + 1) * P], mixed[:, 14 + g, b * P:(b + 1) * P], ident)
                ins.then_inc(v_tr.sem, 1)
            pe.wait_ge(*v_tok.after(1))
            pe.wait_ge(*kv_step.after(1))

            def head(h, stream_on, first=False):
                def run(j, half):
                    if stream_on:
                        stream(h + 1, j, half)

                blk = lambda t, b: t[:, b * P:(b + 1) * P]
                ada_sums(4 + h)
                pe.wait_ge(*gu_made.after(h))
                if not first:
                    pe.wait_ge(*o_taken.after(h - 1))
                for d in range(2):
                    M(pd[3 + d], ones, LL[:, d].rearrange("p b n -> p (b n)"), start=True, stop=True).then_inc(gc_sum.sem, 1)
                run(0, 0)
                run(0, 1)
                run(1, 0)
                if not first:
                    pe.wait_ge(*mix_step.after(h - 1))
                for i, t in enumerate((tmp[:, 0, :], tmp[:, 1, :], sqa)):
                    pe.wait_ge(*sq_done.after(h, i + 1))
                    M(pd[i], ones, t, start=True, stop=True).then_inc(ss_sum.sem, 1)
                run(1, 1)
                k_f, q_f, v_f = act3[:, 0, :], act3[:, 1, :], act3[:, 2, :]
                pe.wait_ge(*norm_made.after(h, 3))
                M(pd[1], rot, qr, start=True, stop=True).then_inc(rot_sum.sem, 1)
                pe.wait_ge(*ada_out.after(4 + h))
                for b in range(NB):
                    ins = M(blk(pd[5], b), blk(k_f, b), blk(k_f, b), start=True, stop=True)
                ins.then_inc(g_sum.sem, 1)
                for b in range(NB):
                    ins = M(blk(pd[0], b), blk(k_f, b), blk(q_f, b), start=True, stop=True)
                ins.then_inc(qk_sum.sem, 1)
                pe.wait_ge(*diff_made.after(h))
                pe.wait_ge(*silu_done.after(h, 3))
                for bank, t in ((pd[3], k_f), (pd[4], v_f)):
                    for b in range(NB):
                        ins = TR(blk(bank, b), blk(t, b), ident)
                    ins.then_inc(tr_sum.sem, 1)
                run(2, 0)

                def scores(b):
                    M(pd[2 - b % 2], blk(qr, b), group(ka, h), start=True, stop=True).then_inc(sc_sum.sem, 1)

                def turn(b):
                    pe.wait_ge(soft_step.sem, 16 * h + SOFT_OUT[b])
                    if b >= 2:
                        pe.wait_ge(*pt_taken.after(h, b - 1))
                    for k in range(NB):
                        ins = TR(blk(pd[3 + b % 2], k), blk(prob[b % 2], k), ident)
                    ins.then_inc(pt_sum.sem, 1)

                pe.wait_ge(*rope_step.after(h))
                scores(0)
                scores(1)
                run(2, 1)
                pe.wait_ge(*tok_done.after(h))
                pe.wait_ge(*p_exp.after(h, 1))
                scores(2)
                turn(0)
                pe.wait_ge(*p_exp.after(h, 2))
                scores(3)
                turn(1)
                run(3, 0)
                turn(2)
                turn(3)
                run(3, 1)
                pe.wait_ge(*pt_taken.after(h))
                pe.wait_ge(*vcur_made.after(h))
                for k in range(NB):
                    ins = M(pd[2], vcur[:, k, :], PT[:, k, :], start=k == 0, stop=k == NB - 1)
                ins.then_inc(av_sum.sem, 1)
                run(4, 0)
                pe.wait_ge(*lm_made.after(h, 1))
                pe.wait_ge(*qk_made.after(h))
                eight = [(d, b) for d in range(2) for b in range(NB)]
                p8 = lambda t, i: t[:, i * P:(i + 1) * P]
                for i in range(8):
                    ins = TR(p8(pd01, i), p8(LMf, i), ident)
                ins.then_inc(lt_sum.sem, 1)
                for n in range(1, LEVELS):
                    pe.wait_ge(*lm_made.after(h, n + 1))
                    if n == 1:
                        pe.wait_ge(*t_first.after(h))
                    else:
                        pe.wait_ge(*t_step.after(h, 2 * (n - 1)))
                    for i in range(8):
                        ins = M(p8(pd01, i), p8(LMf, i), p8(TTf, i), start=True, stop=True)
                    ins.then_inc(y_sum.sem, 1)
                    run(3 + n, 1)
                    pe.wait_ge(*y_taken.after(h, n))
                    if n == 1:
                        pe.wait_ge(*av_taken.after(h))
                    if n < LEVELS - 1:
                        for i in range(8):
                            ins = M(p8(pd23, i), p8(Yf, i), p8(Tf, i), start=True, stop=True)
                        ins.then_inc(a_sum.sem, 1)
                    for i in range(8):
                        ins = M(p8(pd45, i), p8(Tf, i), p8(Yf, i), start=True, stop=True)
                    ins.then_inc(a_sum.sem, 1)
                    run(4 + n, 0)
                pe.wait_ge(*tb_made.after(h, 1))
                for i, (d, b) in enumerate(eight):
                    ins = M(p8(pd01, i), p8(Tf, i), vtok[:, b, :], start=True, stop=True)
                ins.then_inc(u_sum.sem, 1)
                pe.wait_ge(*tb_made.after(h))
                for i, (d, b) in enumerate(eight):
                    ins = M(p8(pd23, i), ktok[:, b, :], p8(TTf, i), start=True, stop=True)
                ins.then_inc(wt_sum.sem, 1)
                run(9, 1)
                pe.wait_ge(*u_taken.after(h))
                pe.wait_ge(*wt_taken.after(h))
                pe.wait_ge(*kd_made.after(h))
                pe.wait_ge(*qd_made.after(h))
                for c in range(NCH):
                    for d in range(2):
                        if c:
                            cc = c if d == 0 else NCH - 1 - c
                            i, r0 = d * NB + cc // 2, DN * (cc % 2)
                            pe.wait_ge(*state_made.after(h, 2 * (c - 1) + d + 1))
                            M(pd[d][r0:r0 + DN, 0:P], Yf[:, i * P + r0:i * P + r0 + DN], st[:, d, :], start=True, stop=True) \
                                .then_inc(vn_sum.sem, 1)
                    for d in range(2):
                        cc = c if d == 0 else NCH - 1 - c
                        i, r0 = d * NB + cc // 2, DN * (cc % 2)
                        r = slice(r0, r0 + DN)
                        o = pd[4 + d][:, cc * DN:(cc + 1) * DN]
                        if c:
                            new = vn[r, d, :]
                            pe.wait_ge(*vnew_made.after(h, 2 * (c - 1) + d + 1))
                            M(o, st[:, d, :], EG[:, d, cc * DN:(cc + 1) * DN], start=True, stop=False)
                        else:
                            new = LLf[r, i * P:(i + 1) * P]
                        ins = M(o, new, DQf[r, i * P + r0:i * P + r0 + DN], start=c == 0, stop=True)
                        if c == NCH - 1:
                            ins.then_inc(o_sum.sem, 1)
                        else:
                            M(pd[d][:, P:2 * P], tmpf[r, i * P:(i + 1) * P], new, start=True, stop=True).then_inc(s_sum.sem, 1)
                pe.wait_ge(*onorm.after(h, 1))
                M(pd[2], ones, tmp[:, 0, :], start=True, stop=True).then_inc(sso_sum.sem, 1)

            head(0, True, first=True)
            with pe.Fori(1, HEADS - 1) as h:
                head(h, True)
            head(HEADS - 1, False)

            pe.wait_ge(*mx_lo.after(0))
            for m in range(2):
                whole(OUT0 // 2 + m, pw[m][:])
            pe.wait_ge(x2_loaded, 16 * NB)
            for m in range(KT):
                if m >= 6:
                    pe.wait_ge(*x2_taken.after(0, m - 5))
                for b in range(NB):
                    ins = TR(pd[m % 6][:, b * P:(b + 1) * P], xtok[:, b, m * P:(m + 1) * P], ident)
                ins.then_inc(x2_sum.sem, 1)
            with pe.Fori(1, KT // 2) as i:
                for j in range(2):
                    pe.wait_ge(out_taken.sem, 2 * i + j - 1)
                    whole(OUT0 // 2 + 2 * i + j, pw[j][:])
            pe.wait_ge(sqacc_step.sem, KT + 1)
            pe.wait_ge(*x2_taken.after(0))
            M(pd[0], ones, sqacc[:], start=True, stop=True).then_inc(ssum.sem, 1)
            pe.wait_ge(*h2_lo.after(0))
            with pe.Fori(0, CHUNKS) as c:
                base = MLP0 // 2 + MLP_PER // 2 * c
                with pe.Fori(0, FC) as f:
                    pe.wait_ge(out_taken.sem, KT * (c + 1))
                    for j in range(2):
                        pe.wait_ge(up_taken.sem, 2 * (FC * c + f) + j + 1)
                        whole(base + 2 * f + j, pw[j][:])
                with pe.Fori(0, KT // 2) as i:
                    pe.wait_ge(up_taken.sem, 2 * FC * (c + 1) + 2)
                    pe.wait_ge(mh_lo_made.sem, FC * (c + 1))
                    for j in range(2):
                        pe.wait_ge(out_taken.sem, KT * (c + 1) + 2 * i + j - 1)
                        whole(base + 2 * FC + 2 * i + j, pw[j][:], (6, FC - 6), mh_hi, mh_lo)
            pe.wait_ge(sqacc_step.sem, 2 * KT + 1)
            M(pd[0], ones, sqacc[:], start=True, stop=True).then_inc(ssum.sem, 1)
            pe.wait_ge(*rstd_step.after(1))
            for i in range(KT):
                b, g = i // 4, i % 4
                if b == 0:
                    pe.wait_ge(*fin_made.after(0, 4 * g + 4))
                if i >= 6:
                    pe.wait_ge(*fin_taken.after(0, i - 5))
                for m in range(4):
                    ins = TR(pd[i % 6][:, m * P:(m + 1) * P], hT[:, 4 * g + m, b * P:(b + 1) * P], ident)
                ins.then_inc(fin_sum.sem, 1)


_INS = ["x", "c", "w_ada", "b_ada", "w_in", "attn_q_norm", "attn_k_norm", "dn_conv_w", "dn_A_log", "dn_dt_bias",
        "dn_norm_w", "w_out", "w_up", "w_ffn_conv", "b_ffn_conv", "w_down", "final_norm"]


def kernel(**inputs):
    import numpy as np
    import concourse.bacc as bacc
    from concourse.bass_utils import run_bass_kernel_spmd

    nc = bacc.Bacc("TRN2", target_bir_lowering=False, num_devices=1)
    arrays = {name: np.ascontiguousarray(inputs[name]) for name in _INS}
    constants, levels = shape_constants(np)
    arrays["shape_constants"], arrays["level_masks"] = constants, levels
    aps, in_map = {}, {}
    for name, a in arrays.items():
        in_map[f"in_{name}_dram"] = a
        aps[name] = nc.dram_tensor(f"in_{name}_dram", a.shape, mybir.dt.from_np(a.dtype), kind="ExternalInput").ap()
    out = nc.dram_tensor("out_dram", (1, S, DM), F32, kind="ExternalOutput").ap()
    build(nc, aps, out)
    r = run_bass_kernel_spmd(nc, [in_map], core_ids=[0])
    return r.results[0]["out_dram"]
```

```python
from contextlib import ExitStack

import concourse.bass as bass
from concourse import mybir

ALU = mybir.AluOpType
ACT = mybir.ActivationFunctionType
AX = mybir.AxisListType
F32 = mybir.dt.float32
F32R = mybir.dt.float32r
BF16 = mybir.dt.bfloat16

P = 128
S = 512
DM = 2048
KT = DM // P
NB = S // P
HEADS = 8
KV_HEADS = 2
DFF = 5632
FT = DFF // P
CHUNKS = 4
FC = FT // CHUNKS
DN = 64
NCH = S // DN
EPS = 1e-6
BIG = 1e30
UK = 8
ADA_W = 1024
ADA_SLOTS = 4
ADA_STEPS = 6 * DM // ADA_W

COL_QA, COL_KA, COL_VA = 0, 1024, 1280
COL_Q, COL_K, COL_V, COL_Z, COL_BA = 1536, 2560, 3584, 4608, 5632

C_ID, C_ONE, C_ROT = 0, 128, 256
C_CUM, C_REST = 384, 640
C_ML, C_MQ = 896, 1152
C_COS, C_SIN = 1408, 1920
C_EPS = 2432
C_ZERO = 2434
C_N = 2436
SOFT_MAX = [2, 4, 8, 12]
SOFT_OUT = [6, 10, 14, 16]
LEVELS = 6

V_BADA, V_QN, V_KN, V_DNW, V_FN = 0, 96, 97, 98, 99
V_CONV = 115
V_FCONV = V_CONV + 72
V_FB = V_FCONV + 264
V_N = V_FB + 88
ADA_ORDER = (0, 2, 1, 3)


def shape_constants(np):
    c = np.zeros((P, C_N), np.float32)
    p, f = np.arange(P)[:, None], np.arange(P)[None, :]
    same = p // DN == f // DN
    c[:, C_ID:C_ID + P] = p == f
    c[:, C_ONE:C_ONE + P] = 1.0
    quarter = P // 4
    c[:, C_ROT:C_ROT + P] = ((f // quarter) % 2 == 1) & (p == f - quarter)
    c[:, C_ROT:C_ROT + P] -= ((f // quarter) % 2 == 0) & (p == f + quarter)
    for d, (upto, after) in enumerate(((p <= f, p > f), (p >= f, p < f))):
        c[:, C_CUM + d * P:C_CUM + (d + 1) * P] = same & upto
        c[:, C_REST + d * P:C_REST + (d + 1) * P] = same & after
        c[:, C_ML + d * P:C_ML + (d + 1) * P] = np.where(same & after, 0.0, BIG)
        c[:, C_MQ + d * P:C_MQ + (d + 1) * P] = np.where(same & upto, 0.0, BIG)
    t = np.arange(S)
    inv = (np.float32(10000.0) ** (-np.arange(0, P // 2, 2, dtype=np.float32) / np.float32(P // 2))).astype(np.float32)
    for half, where in enumerate((t // 64, t % 64)):
        angle = where.astype(np.float32)[None, :] * inv[:, None]
        for q in range(2):
            rows = slice(half * 64 + q * 32, half * 64 + q * 32 + 32)
            c[rows, C_COS:C_COS + S] = np.cos(angle)
            c[rows, C_SIN:C_SIN + S] = np.sin(angle)
    c[:, C_EPS] = EPS
    c[:, C_EPS + 1] = EPS * P
    m = np.zeros((P, LEVELS, 2, P), np.float32)
    for n in range(LEVELS):
        b = 1 << n
        pair = p // (2 * b) == f // (2 * b)
        m[:, n, 0] = pair & ((p // b) % 2 == 1) & ((f // b) % 2 == 0)
        m[:, n, 1] = pair & ((p // b) % 2 == 0) & ((f // b) % 2 == 1)
    return c, m.reshape(P, -1)


class Signal:

    def __init__(self, sem, per):
        self.sem, self.per = sem, per

    def after(self, i, k=None):
        return self.sem, i * self.per + (self.per if k is None else k)


def build(nc, A, out):
    ctx = ExitStack()
    with ctx:
        def sb(name, shape, dt=F32, where=ctx):
            return where.enter_context(nc.sbuf_tensor(name, shape, dt))

        def sem(name):
            return ctx.enter_context(nc.semaphore(name))

        def signal(name, per=1):
            return Signal(sem(name), per)

        act_hi = sb("act_hi", [P, KT, S], F32R)
        for_float32 = ExitStack()
        x_feat = sb("x_feat", [P, KT, S], F32, for_float32)
        for_float32.close()
        otok = sb("otok", [P, NB, DM], F32, for_float32)
        for_float32.close()
        act_lo = sb("act_lo", [P, KT, S], F32R)
        raw = [sb(f"raw{i}", [P, UK, P]) for i in range(2)]
        w_hi = [sb(f"w_hi{i}", [P, UK, P], F32R) for i in range(2)]
        w_lo = [sb(f"w_lo{i}", [P, UK, P], F32R) for i in range(2)]
        cst = sb("cst_sb", [P, C_N])
        col = sb("col", [P, V_N])
        mod = sb("mod", [P, 6 * KT])
        cond = sb("cond", [P, KT])
        nrm = sb("nrm", [P, 3, NB])

        start = ExitStack()
        wba_hi = sb("wba_hi", [P, KT, 32], F32R, start)
        wba_lo = sb("wba_lo", [P, KT, 32], F32R, start)
        start.close()
        mixer = ExitStack()
        ka = sb("ka", [P, KV_HEADS, S], F32, mixer)
        va = sb("va", [P, KV_HEADS, S], F32, mixer)
        mixed = sb("mixed", [P, 2 * HEADS, S], F32, mixer)
        ada_w = [sb(f"ada_w{i}", [P, ADA_W], F32, mixer) for i in range(2)]
        ada_acc = sb("ada_acc", [P, ADA_W], F32, mixer)
        lvl = sb("lvl", [P, LEVELS, 2, P], BF16, mixer)
        pre = sb("pre", [P, 3, S + 2], F32, mixer)
        act3 = sb("act3", [P, 3, S], F32, mixer)
        tmp = sb("tmp", [P, 2, S], F32, mixer)
        ktok = sb("ktok", [P, NB, P], F32, mixer)
        vtok = sb("vtok", [P, NB, P], F32, mixer)
        LL = sb("LL", [P, 2, NB, P], F32, mixer)
        DQ = sb("DQ", [P, 2, NB, P], F32, mixer)
        EG = sb("EG", [P, 2, S], F32, mixer)
        TT = sb("TT", [P, 2, NB, P], F32, mixer)
        T = sb("T", [P, 2, NB, P], F32, mixer)
        YL = sb("YL", [P, 2, 2, NB, P], F32, mixer)
        vn = sb("vn", [P, 2, P], F32, mixer)
        st = sb("st", [P, 2, P], F32, mixer)
        gall = sb("gall", [P, 5, NB, 2, HEADS], F32, mixer)
        gcur = sb("gcur", [P, 5, NB, 2], F32, mixer)
        glast = sb("glast", [P, 2, NCH], F32, mixer)
        soft = sb("soft", [P, 4, NB], F32, mixer)
        gates = sb("gates", [P, 2, 16], F32, mixer)
        mixer.close()
        two = lambda t: t[:].rearrange("p d b n -> p (d b n)")
        LLf, DQf, TTf, Tf = two(LL), two(DQ), two(TT), two(T)
        EGf = EG[:].rearrange("p d n -> p (d n)")
        Yf = YL[:, 0].rearrange("p d b n -> p (d b n)")
        LMf = YL[:, 1].rearrange("p d b n -> p (d b n)")
        LM = YL[:, 1]
        ktf = ktok[:].rearrange("p b n -> p (b n)")
        vtf = vtok[:].rearrange("p b n -> p (b n)")
        tmpf = tmp[:].rearrange("p d n -> p (d n)")
        mixedf = mixed[:].rearrange("p t n -> p (t n)")
        qr, vcur = TTf[:, 0:S], TTf[:, S:2 * S].rearrange("p (b n) -> p b n", n=P)
        prob = [Tf[:, 0:S], Tf[:, S:2 * S]]
        sqa, rotsin = Yf[:, 0:S], Yf[:, S:2 * S]
        PT = YL[:].rearrange("p a d b n -> p (a d b n)").rearrange("p (k q) -> p k q", q=S)
        x_in = mixed[:].rearrange("p t n -> p (t n)").rearrange("p (b n) -> p b n", n=DM)
        wba = Tf[:, 0:512].rearrange("p (k n) -> p k n", n=32)
        ada_first = [LLf, DQf, EGf, TTf]
        junk = YL[:].rearrange("p a d b n -> p (a d b n)")
        rows = pre[:].rearrange("p t n -> p (t n)")[:, 0:6 * P].rearrange("p (t n) -> p t n", n=P)
        arow = vn[0:1, 0, 0:32]
        lvl_f32 = [ktf, vtf, act3[:, 1, :]]
        hn_tmp = [tmp[:, 0, :], tmp[:, 1, :]]

        mlp = ExitStack()
        mh_hi = sb("mh_hi", [P, FC, S], F32R, mlp)
        mh_lo = sb("mh_lo", [P, FC, S], F32R, mlp)
        rstd = sb("rstd", [P, S], F32, mlp)
        gp = sb("gp", [P, 2, S + 2], F32, mlp)
        cv = sb("cv", [P, 2, S], F32, mlp)
        prod = sb("prod", [P, S], F32, mlp)
        hn2 = sb("hn2", [P, 2, S], F32, mlp)
        sb("apart", [P, 258], F32, mlp)
        hT = sb("hT", [P, KT, S], F32, mlp)
        sqacc = sb("sqacc", [P, S], F32, mlp)
        sq = sb("sq", [P, S], F32, mlp)
        mlp.close()
        X_SLOTS = 4
        xs = ctx.enter_context(nc.sbuf_tensor("xs", [P, X_SLOTS, NB, P], F32))
        sums = [mixed[:, t, :] for t in range(0, 2 * HEADS, 2)]
        sums += [w[:, i * S:(i + 1) * S] for w in (*ada_w, ada_acc) for i in range(2)] + [pre[:, i, 0:S] for i in range(2)]
        OUT_TILES = (range(0, KT, 2), range(1, KT, 2))
        hTf = hT[:].rearrange("p t n -> p (t n)")
        mhf_hi = mh_hi[:].rearrange("p t n -> p (t n)")
        mhf_lo = mh_lo[:].rearrange("p t n -> p (t n)")

        pw = [ctx.enter_context(nc.psum_tensor(f"pw{i}", [P, S], F32)) for i in range(2)]
        pdt = ctx.enter_context(nc.psum_tensor("pd", [P, 6, S], F32))
        pd = [pdt[:, i, :] for i in range(6)]
        pd01 = pdt[:, 0:2, :].rearrange("p a n -> p (a n)")
        pd23 = pdt[:, 2:4, :].rearrange("p a n -> p (a n)")
        pd34 = pdt[:, 3:5, :].rearrange("p a n -> p (a n)")
        pd45 = pdt[:, 4:6, :].rearrange("p a n -> p (a n)")
        ident = cst[:, C_ID:C_ID + P]
        ones = cst[:, C_ONE:C_ONE + P]
        rot = cst[:, C_ROT:C_ROT + P]
        cosT, sinT = cst[:, C_COS:C_COS + S], cst[:, C_SIN:C_SIN + S]
        eps1, eps128 = cst[:, C_EPS:C_EPS + 1], cst[:, C_EPS + 1:C_EPS + 2]

        w_in, w_out, w_up, w_down = A["w_in"][0], A["w_out"][0], A["w_up"][0], A["w_down"][0]

        KV0, HEAD0 = 0, 8
        OUT0 = HEAD0 + 10 * HEADS
        MLP0 = OUT0 + 2 * KT
        MLP_PER = 4 * FC + 2 * KT
        raw_in = [sem(f"raw_in{i}") for i in range(2)]
        hi_made = signal("hi_made")
        lo_made = signal("lo_made")
        unit_used = signal("unit_used")
        tile_taken = signal("tile_taken")
        out_taken = signal("out_taken")
        up_taken = signal("up_taken")

        consts_in, x_loaded, rows_in, c_in = sem("consts_in"), sem("x_loaded"), sem("rows_in"), sem("c_in")
        x2_in, stored, ba_in, small_in = [sem(f"x2_in{i}") for i in range(X_SLOTS)], sem("stored"), sem("ba_in"), sem("small_in")
        lvl_in = [sem(f"lvl_in{i}") for i in range(3)]
        ada_in0 = [sem(f"ada_first_in{i}") for i in range(4)]
        ada_in = [sem(f"ada_in{i}") for i in range(2)]
        ada_step = signal("ada_step", KT)
        ada_sum = signal("ada_sum")
        ada_out = signal("ada_out")

        block = ctx.enter_context(nc.Block())

        conv_step = signal("conv_step", 9)
        gcur_made = signal("gcur_made", 1)
        gu_made = signal("gu_made", 2)
        diff_made = signal("diff_made", 2)
        dq_masked = signal("dq_masked", 1)
        ll_masked = signal("ll_masked", 1)
        norm_made = signal("norm_made", 3)
        rot_scaled = signal("rot_scaled", 1)
        rope_step = signal("rope_step", 2)
        ll_step = signal("ll_step", 2)
        qk_made = signal("qk_made", 1)
        soft_step = signal("soft_step", 4 * NB)
        av_taken = signal("av_taken", 1)
        t_first = signal("t_first", 2)
        t_step = signal("t_step", 9)
        tb_made = signal("tb_made", 2)
        wt_taken = signal("wt_taken", 1)
        kd_made = signal("kd_made", 1)
        gl_made = signal("gl_made", 2)
        qd_made = signal("qd_made", 1)
        vnew_made = signal("vnew_made", 2 * (NCH - 1))
        state_made = signal("state_made", 2 * (NCH - 1))
        o_summed = signal("o_summed", 1)
        mix_step = signal("mix_step", 2)
        silu_done = signal("silu_done", 4)
        sq_done = signal("sq_done", 3)
        eg_done = signal("eg_done", 1)
        ln_done = signal("ln_done", 3)
        rstd_made = signal("rstd_made", 3)
        decay_done = signal("decay_done", 2)
        tok_done = signal("tok_done", 2)
        p_exp = signal("p_exp", NB)
        pt_taken = signal("pt_taken", NB)
        y_taken = signal("y_taken", LEVELS - 1)
        u_taken = signal("u_taken", 1)
        o_taken = signal("o_taken", 1)
        onorm = signal("onorm", 3)
        gc_sum = signal("gc_sum", 2)
        ss_sum = signal("ss_sum", 3)
        tr_sum = signal("tr_sum", 2)
        g_sum = signal("g_sum", 1)
        qk_sum = signal("qk_sum", 1)
        rot_sum = signal("rot_sum", 1)
        sc_sum = signal("sc_sum", NB)
        pt_sum = signal("pt_sum", NB)
        av_sum = signal("av_sum", 1)
        lt_sum = signal("lt_sum", 1)
        y_sum = signal("y_sum", LEVELS - 1)
        a_sum = signal("a_sum", 9)
        u_sum = signal("u_sum", 1)
        wt_sum = signal("wt_sum", 1)
        vn_sum = signal("vn_sum", 2 * (NCH - 1))
        s_sum = signal("s_sum", 2 * (NCH - 1))
        o_sum = signal("o_sum", 2)
        sso_sum = signal("sso_sum", 1)
        lm_made = signal("lm_made", LEVELS)
        vcur_made = signal("vcur_made", 1)

        cols_sum, cols_made, cond_made = signal("cols_sum"), signal("cols_made", 2), signal("cond_made")
        more_in, c_sum, x_turned = sem("more_in"), signal("c_sum"), signal("x_turned", KT)
        ba_split, ba_row_sum, ba_row_taken = signal("ba_split", 2), signal("ba_row_sum"), signal("ba_row_taken")
        gate_row_sum, gates_made = signal("gate_row_sum"), signal("gates_made", 2)
        x_squared, x_rstd = signal("x_squared", NB), signal("x_rstd", 2)
        x_normed, xt_sum = signal("x_normed", NB), signal("xt_sum", KT)
        hn_full, hn_hi, hn_lo = signal("hn_full", KT), signal("hn_hi", KT), signal("hn_lo", KT)
        lvl_made, pads_made = signal("lvl_made", 3), signal("pads_made", 2)
        scale_made = signal("scale_made", 2)
        ba_sum, cum_sum = signal("ba_sum"), signal("cum_sum")
        gate_a, gate_v = signal("gate_a", 6), signal("gate_v", 7)
        kv_sq, kv_ss, kv_rstd = signal("kv_sq", 1), signal("kv_ss", 1), signal("kv_rstd", 2)
        kv_step, kv_rot = signal("kv_step", 4), signal("kv_rot", 1)
        v_tr, v_tok = signal("v_tr", 1), signal("v_tok", 1)

        sums_taken, sums_added = signal("sums_taken"), signal("sums_added", KT)
        mx_hi, mx_lo = signal("mx_hi", KT), signal("mx_lo", KT)
        x2_sum, x2_taken = signal("x2_sum", KT), signal("x2_taken", KT)
        sq_made, sq_added = signal("sq_made", KT), signal("sq_added", KT)
        ssum, rstd_step, scale2_made = signal("ssum"), signal("rstd_step", 2), signal("scale2_made")
        sqacc_step = signal("sqacc_step")
        h2_step, h2_hi, h2_lo = signal("h2_step", KT), signal("h2_hi", KT), signal("h2_lo", KT)
        sqacc_again = signal("sqacc_again")
        fconv_step = signal("fconv_step", 6)
        fsilu, fprod = signal("fsilu"), signal("fprod")
        mh_hi_made, mh_lo_made = signal("mh_hi_made"), signal("mh_lo_made")
        fin_made, fin_sum, fin_taken = signal("fin_made"), signal("fin_sum"), signal("fin_taken")
        scaled_v, scaled_a = signal("scaled_v"), signal("scaled_a")

        SCALE = float(P) ** -0.5
        TAPS = 3

        @block.sync
        def _(sp):
            sp.dma_start(cst[:, 0:2 * P], A["shape_constants"][:, 0:2 * P]).then_inc(consts_in, 16)
            sp.dma_start(rows[0:16, 5, :], A["c"].rearrange("o (n p) -> (o n) p", p=P)).then_inc(c_in, 16)
            for b in range(NB):
                sp.dma_start(x_in[:, b, :], A["x"][0, b * P:(b + 1) * P, :]).then_inc(x_loaded, 16)
            sp.dma_start(cst[:, 2 * P:C_N], A["shape_constants"][:, 2 * P:C_N]).then_inc(more_in, 16)
            sp.dma_start(wba, w_in[:, COL_BA:COL_BA + 32].rearrange("(k p) n -> p k n", p=P)).then_inc(ba_in, 16)

            def load(slot, u, src, n_k, first=False):
                if not first:
                    sp.wait_ge(lo_made.sem, u - 1)
                sp.dma_start(raw[slot][:, 0:n_k, :], src.rearrange("(k p) n -> p k n", p=P)).then_inc(raw_in[slot], 16)

            def tile(u, w, column, first=False):
                for j in range(2):
                    load(j, u + j, w[j * UK * P:(j + 1) * UK * P, bass.ds(column, P)], UK, first)

            for t, c0 in enumerate((COL_KA, COL_KA + P, COL_VA, COL_VA + P)):
                tile(KV0 + 2 * t, w_in, c0, first=t == 0)
            with sp.Fori(1, HEADS + 1) as after:
                for t, c0 in enumerate((COL_K, COL_Q, COL_V, COL_QA, COL_Z)):
                    tile(HEAD0 - 10 + 10 * after + 2 * t, w_in, after * P + (c0 - P))
            out_rows = w_out.rearrange("(k g p) n -> g p k n", g=2, p=P)
            for g in range(2):
                with sp.Fori(0, KT // 2) as i:
                    for j in range(2):
                        sp.wait_ge(lo_made.sem, OUT0 + KT * g - 1 + 2 * i + j)
                        sp.dma_start(raw[j][:], out_rows[g][:, :, bass.ds((2 * i + j) * P, P)]).then_inc(raw_in[j], 16)
            with sp.Fori(0, CHUNKS) as c:
                with sp.Fori(0, FC) as f:
                    for part in range(2):
                        tile(MLP0 + MLP_PER * c + 4 * f + 2 * part, w_up, part * DFF + (c * FC + f) * P)
                with sp.Fori(0, KT) as m:
                    u = MLP0 + MLP_PER * c + 4 * FC + 2 * m
                    for j, (k0, n_k) in enumerate(((0, 6), (6, FC - 6))):
                        load(j, u + j, w_down[bass.ds((c * FC + k0) * P, n_k * P), bass.ds(m * P, P)], n_k)
            for j in range(2):
                load(j, MLP0 + CHUNKS * MLP_PER + j, w_down[0:UK * P, 0:P], UK)
            half = DM // 2
            for b in range(NB):
                for i, scaled in enumerate((scaled_v, scaled_a)):
                    sp.wait_ge(scaled.sem, b + 1)
                    sp.dma_start(out[0, b * P:(b + 1) * P, i * half:(i + 1) * half], otok[:, b, i * half:(i + 1) * half]) \
                        .then_inc(stored, 16)
            sp.wait_ge(stored, 2 * 16 * NB)

        def group(t, h):
            return t[:].rearrange("p g n -> p (g n)")[:, bass.ds((h & 4) * (S // 4), S)]

        def at(t, i, width=S):
            return t[:, bass.ds(i * width, width)]

        @block.gpsimd
        def _(pool):
            for j in range(4):
                for k in range(KT):
                    n = j * KT + k
                    if n >= 4:
                        pool.wait_ge(ada_step.sem, n - 3)
                    pool.dma_start(ada_first[k % 4], A["w_ada"][0, k * P:(k + 1) * P, ADA_ORDER[j] * ADA_W:(ADA_ORDER[j] + 1) * ADA_W]) \
                        .then_inc(ada_in0[k % 4], 16)
            pool.wait_ge(*cols_made.after(0))
            nc.gpsimd.memset(pre[:, :, 0:1], 0.0).then_inc(pads_made.sem, 1)
            nc.gpsimd.memset(pre[:, :, S + 1:S + 2], 0.0).then_inc(pads_made.sem, 1)

            def ada_loads(h, g, first=False):
                for k in range(2 * g, 2 * g + 2):
                    if not (first and g == 0):
                        pool.wait_ge(ada_step.sem, (4 + h) * KT + k - 1)
                    pool.dma_start(ada_w[k % 2][:], A["w_ada"][0, k * P:(k + 1) * P, bass.ds((4 + h) * ADA_W, ADA_W)]) \
                        .then_inc(ada_in[k % 2], 16)

            def head(h, stream):
                if stream:
                    ada_loads(h + 1, 0)
                pool.wait_ge(*norm_made.after(h, 3))
                nc.gpsimd.tensor_copy(vcur.rearrange("p b n -> p (b n)"), group(va, h)).then_inc(vcur_made.sem, 1)
                if stream:
                    ada_loads(h + 1, 1)
                for n in range(LEVELS):
                    if n == 0:
                        pool.wait_ge(*ll_step.after(h))
                        pool.wait_ge(*av_sum.after(h))
                    elif n == 1:
                        pool.wait_ge(*t_first.after(h))
                        pool.wait_ge(*lt_sum.after(h))
                    else:
                        pool.wait_ge(*y_sum.after(h, n - 1))
                    mask = lvl[:, n].unsqueeze(2).broadcast_to([P, 2, NB, P])
                    nc.gpsimd.tensor_tensor(LM, LL[:], mask, ALU.mult).then_inc(lm_made.sem, 1)
                    if stream:
                        ada_loads(h + 1, 2 + n)

            for g in range(8):
                ada_loads(0, g, first=True)
            pool.wait_ge(*v_tok.after(1))
            head(0, True)
            with pool.Fori(1, HEADS - 1) as h:
                head(h, True)
            head(HEADS - 1, False)
            pool.wait_ge(*sc_sum.after(HEADS - 1))
            x_rows = A["x"][0].rearrange("(b p) n -> p b n", p=P)
            for m in range(KT):
                if m >= X_SLOTS:
                    pool.wait_ge(*x2_sum.after(0, m - X_SLOTS + 1))
                pool.dma_start(xs[:, m % X_SLOTS], x_rows[:, :, m * P:(m + 1) * P]).then_inc(x2_in[m % X_SLOTS], 16)

        @block.scalar
        def _(act):
            for dst, src in ((rows[0:96, 0, :], A["b_ada"][0].rearrange("(n p) -> n p", p=P)),
                             (rows[96:97, 0, :], A["attn_q_norm"]),
                             (rows[97:98, 0, :], A["attn_k_norm"]),
                             (rows[98:99, 0, :], A["dn_norm_w"]),
                             (rows[99:115, 0, :], A["final_norm"].rearrange("(n p) -> n p", p=P)),
                             (rows[0:72, 1, :], A["dn_conv_w"][0].rearrange("t (n p) -> (t n) p", p=P)),
                             (rows[0:128, 2, :], A["w_ffn_conv"][0].rearrange("t (n p) -> (t n) p", p=P)[0:128]),
                             (rows[0:128, 3, :], A["w_ffn_conv"][0].rearrange("t (n p) -> (t n) p", p=P)[128:256]),
                             (rows[0:8, 4, :], A["w_ffn_conv"][0].rearrange("t (n p) -> (t n) p", p=P)[256:264]),
                             (rows[8:96, 4, :], A["b_ffn_conv"][0].rearrange("(n p) -> n p", p=P))):
                act.dma_start(dst, src).then_inc(rows_in, 16)
            act.dma_start(arow[:, 0:16], A["dn_dt_bias"].rearrange("o d h -> o (d h)")).then_inc(small_in, 16)
            act.dma_start(arow[:, 16:32], A["dn_A_log"].rearrange("o d h -> o (d h)")).then_inc(small_in, 16)
            for i in range(3):
                act.dma_start(lvl_f32[i], A["level_masks"][:, i * S:(i + 1) * S]).then_inc(lvl_in[i], 16)

            def split(q, slot, ahead=True):
                act.wait_ge(raw_in[slot], 16 * (q + 1))
                if ahead:
                    act.wait_ge(unit_used.sem, 2 * q + slot - 1)
                nc.scalar.activation(w_hi[slot][:], raw[slot][:], ACT.Copy).then_inc(hi_made.sem, 1)

            def evacuate(h, t, first=False):
                act.wait_ge(unit_used.sem, HEAD0 + 10 * h + 2 * t + 2)
                if t < 3:
                    if not first:
                        act.wait_ge(conv_step.sem, 9 * h - 9 + 3 * (t + 1))
                    dst = pre[:, t, 1:S + 1]
                else:
                    dst = at(mixedf, h if t == 3 else HEADS + h)
                nc.scalar.activation(dst, pw[t % 2][:], ACT.Copy).then_inc(tile_taken.sem, 1)

            act.wait_ge(*c_sum.after(0))
            nc.scalar.activation(cond[:], pd[3][:, 0:KT], ACT.Silu).then_inc(cond_made.sem, 1)
            act.wait_ge(*gate_row_sum.after(0))
            nc.scalar.activation(gates[:, 0, :], pd[2][:, 0:16], ACT.Copy).then_inc(gates_made.sem, 1)
            nc.scalar.activation(gates[:, 1, :], pd[2][:, 16:32], ACT.Exp).then_inc(gates_made.sem, 1)
            act.wait_ge(x_loaded, 16 * NB)
            for b in range(NB):
                if b:
                    act.wait_ge(*x_squared.after(0, b))
                nc.scalar.activation(junk, x_in[:, b, :], ACT.Square, accum_out=nrm[:, 0, b:b + 1]).then_inc(x_squared.sem, 1)
            act.wait_ge(*x_squared.after(0))
            act.wait_ge(more_in, 16)
            nc.scalar.activation(nrm[:, 1, :], nrm[:, 0, :], ACT.Ln, scale=1.0 / DM, bias=eps1).then_inc(x_rstd.sem, 1)
            act.wait_ge(*x_rstd.after(0, 1))
            nc.scalar.activation(nrm[:, 2, :], nrm[:, 1, :], ACT.Exp, scale=-0.5).then_inc(x_rstd.sem, 1)
            act.wait_ge(*x_rstd.after(0))
            for b in range(NB):
                nc.scalar.activation(x_in[:, b, :], x_in[:, b, :], ACT.Identity, scale=nrm[:, 2, b:b + 1]) \
                    .then_inc(x_normed.sem, 1)
            for m in range(KT):
                act.wait_ge(*xt_sum.after(0, m + 1))
                nc.scalar.activation(x_feat[:, m, :], pd[m % 4], ACT.Copy).then_inc(x_turned.sem, 1)
            act.wait_ge(ba_in, 16)
            nc.scalar.activation(wba_hi[:], wba, ACT.Copy).then_inc(ba_split.sem, 1)
            split(0, 0, ahead=False)
            split(0, 1, ahead=False)
            act.wait_ge(*x_turned.after(0))
            for m in range(KT):
                act.wait_ge(*scale_made.after(0, 1 + m // 8))
                nc.scalar.activation(act_hi[:, m, :], x_feat[:, m, :], ACT.Identity, scale=mod[:, 16 + m:17 + m],
                                     bias=mod[:, m:m + 1]).then_inc(hn_hi.sem, 1)

            def kv_tile(t):
                split(t + 1, 0)
                act.wait_ge(unit_used.sem, 2 * t + 2)
                nc.scalar.activation(mixed[:, 12 + t, :], pw[t % 2][:], ACT.Copy).then_inc(tile_taken.sem, 1)
                split(t + 1, 1)

            kv_tile(0)
            act.wait_ge(*ba_row_sum.after(0))
            nc.scalar.activation(tmp[0:32, 0, :], pd[4][0:32, :], ACT.Copy).then_inc(ba_row_taken.sem, 1)
            kv_tile(1)
            act.wait_ge(*ba_sum.after(0))
            nc.scalar.activation(gall[:, 0], pd[4][:, 0:128].rearrange("p (b n) -> p b n", n=32)[:, :, 0:16], ACT.Exp,
                                 scale=-1.0).then_inc(gate_a.sem, 1)
            act.wait_ge(*gate_v.after(0, 1))
            nc.scalar.activation(tmpf[:, 64:128], tmpf[:, 0:64], ACT.Abs).then_inc(gate_a.sem, 1)
            act.wait_ge(*gate_a.after(0, 2))
            nc.scalar.activation(tmpf[:, 64:128], tmpf[:, 64:128], ACT.Exp, scale=-1.0).then_inc(gate_a.sem, 1)
            act.wait_ge(*gate_a.after(0, 3))
            nc.scalar.activation(tmpf[:, 64:128], tmpf[:, 64:128], ACT.Ln, bias=1.0).then_inc(gate_a.sem, 1)
            kv_tile(2)
            act.wait_ge(*cum_sum.after(0))
            nc.scalar.activation(gall[:, 3], pd[3][:, 64:128], ACT.Exp).then_inc(gate_a.sem, 1)
            nc.scalar.activation(tmpf[:, 128:192], pd[3][:, 0:64], ACT.Exp).then_inc(gate_a.sem, 1)

            kv_tile(3)
            act.wait_ge(*pads_made.after(0))
            for t in range(5):
                split(HEAD0 // 2 + t + 1, 0)
                if t < KV_HEADS:
                    act.wait_ge(tile_taken.sem, 4)
                    if t:
                        act.wait_ge(kv_step.sem, 4 * t)
                    nc.scalar.activation(sqa, mixed[:, 12 + t, :], ACT.Square).then_inc(kv_sq.sem, 1)
                evacuate(0, t, first=True)
                if t < KV_HEADS:
                    act.wait_ge(*kv_ss.after(t))
                    nc.scalar.activation(sqa, pd[2], ACT.Ln, scale=1.0 / P, bias=eps1).then_inc(kv_rstd.sem, 1)
                    act.wait_ge(*kv_rstd.after(t, 1))
                    nc.scalar.activation(sqa, sqa, ACT.Exp, scale=-0.5).then_inc(kv_rstd.sem, 1)
                    act.wait_ge(*v_tr.after(t))
                    nc.scalar.activation(va[:, t, :], pd[3], ACT.Copy).then_inc(v_tok.sem, 1)
                if t < 4:
                    split(HEAD0 // 2 + t + 1, 1)

            def halves(g):
                for t in OUT_TILES[g]:
                    nc.scalar.activation(act_hi[:, t, :], mixed[:, t, :], ACT.Copy).then_inc(mx_hi.sem, 1)

            def take_sum(m):
                act.wait_ge(unit_used.sem, OUT0 + m + 1)
                nc.scalar.activation(sums[m], pw[m % 2][:], ACT.Copy).then_inc(sums_taken.sem, 1)

            def head(h, stream, first=False, out=False):
                def s(head_, j):
                    split(HEAD0 // 2 + 5 * head_ + (j + 1) // 2, (j + 1) % 2)
                    if out and j:
                        take_sum(j - 1)

                def evacuate_next(t):
                    if not out:
                        evacuate(h + 1, t)

                if stream:
                    s(h + 1, 0)
                if out:
                    act.wait_ge(unit_used.sem, OUT0)
                    act.wait_ge(*mix_step.after(h - 1))
                    act.wait_ge(*av_taken.after(h - 1))
                    halves(0)
                if not first:
                    act.wait_ge(*mix_step.after(h - 1))
                act.wait_ge(tile_taken.sem, 4 + 5 * h + 5)
                for part, sq_to in ((0, tmp[:, 0, :]), (1, tmp[:, 1, :])):
                    act.wait_ge(*conv_step.after(h, 3 * (part + 1)))
                    nc.scalar.activation(act3[:, part, :], act3[:, part, :], ACT.Silu).then_inc(silu_done.sem, 1)
                    act.wait_ge(*silu_done.after(h, part + 1))
                    nc.scalar.activation(sq_to, act3[:, part, :], ACT.Square).then_inc(sq_done.sem, 1)
                nc.scalar.activation(sqa, at(mixedf, h), ACT.Square).then_inc(sq_done.sem, 1)
                act.wait_ge(*conv_step.after(h))
                nc.scalar.activation(act3[:, 2, :], act3[:, 2, :], ACT.Silu).then_inc(silu_done.sem, 1)
                nc.scalar.activation(at(mixedf, HEADS + h), at(mixedf, HEADS + h), ACT.Silu).then_inc(silu_done.sem, 1)
                act.wait_ge(*gc_sum.after(h))
                nc.scalar.activation(EGf, pd34, ACT.Exp).then_inc(eg_done.sem, 1)
                if stream:
                    s(h + 1, 1)
                for i, (to, scale, eps) in enumerate(((tmp[:, 0, :], 1.0, eps1), (tmp[:, 1, :], float(P), eps128),
                                                      (sqa, 1.0 / P, eps1))):
                    act.wait_ge(*ss_sum.after(h, i + 1))
                    nc.scalar.activation(to, pd[i], ACT.Ln, scale=scale, bias=eps).then_inc(ln_done.sem, 1)
                for i, to in enumerate((tmp[:, 0, :], tmp[:, 1, :], sqa)):
                    act.wait_ge(*ln_done.after(h, i + 1))
                    nc.scalar.activation(to, to, ACT.Exp, scale=-0.5).then_inc(rstd_made.sem, 1)
                if stream:
                    evacuate_next(0)
                    s(h + 1, 2)
                act.wait_ge(*ll_masked.after(h))
                nc.scalar.activation(LLf, LLf, ACT.Exp, scale=-1.0).then_inc(decay_done.sem, 1)
                nc.scalar.activation(DQf, DQf, ACT.Exp).then_inc(decay_done.sem, 1)
                for i, (to, bank) in enumerate(((ktf, pd[3]), (vtf, pd[4]))):
                    act.wait_ge(*tr_sum.after(h, i + 1))
                    nc.scalar.activation(to, bank, ACT.Copy).then_inc(tok_done.sem, 1)

                def weigh(b):
                    act.wait_ge(soft_step.sem, 4 * NB * h + SOFT_MAX[b])
                    nc.scalar.activation(prob[b % 2], pd[2 - b % 2], ACT.Exp, scale=SCALE, bias=soft[:, 1, b:b + 1],
                                         accum_out=soft[:, 2, b:b + 1]).then_inc(p_exp.sem, 1)

                def turned(b):
                    act.wait_ge(*pt_sum.after(h, b + 1))
                    nc.scalar.activation(PT[:, :, b * P:(b + 1) * P], pd[3 + b % 2].rearrange("p (k q) -> p k q", q=P),
                                         ACT.Copy).then_inc(pt_taken.sem, 1)

                weigh(0)
                weigh(1)
                if stream:
                    s(h + 1, 3)
                turned(0)
                act.wait_ge(*pt_sum.after(h, 1))
                weigh(2)
                turned(1)
                weigh(3)
                turned(2)
                turned(3)
                if stream:
                    evacuate_next(1)
                if stream:
                    s(h + 1, 4)
                for n in range(1, LEVELS):
                    act.wait_ge(*y_sum.after(h, n))
                    nc.scalar.activation(Yf, pd01, ACT.Copy).then_inc(y_taken.sem, 1)
                    if stream:
                        s(h + 1, 4 + n)
                        if n in (2, 4):
                            evacuate_next(2 + (n == 4))
                act.wait_ge(*u_sum.after(h))
                nc.scalar.activation(LLf, pd01, ACT.Copy).then_inc(u_taken.sem, 1)
                if stream:
                    evacuate_next(4)
                act.wait_ge(*o_sum.after(h, 1))
                nc.scalar.activation(act3[:, 1, :], pd[4], ACT.Copy).then_inc(o_taken.sem, 1)
                act.wait_ge(*o_summed.after(h))
                nc.scalar.activation(tmp[:, 0, :], act3[:, 1, :], ACT.Square).then_inc(onorm.sem, 1)
                act.wait_ge(*sso_sum.after(h))
                nc.scalar.activation(tmp[:, 1, :], pd[2], ACT.Ln, scale=1.0 / P, bias=eps1).then_inc(onorm.sem, 1)
                act.wait_ge(*onorm.after(h, 2))
                nc.scalar.activation(tmp[:, 1, :], tmp[:, 1, :], ACT.Exp, scale=-0.5).then_inc(onorm.sem, 1)

            head(0, True, first=True)
            with act.Fori(1, HEADS - 1) as h:
                head(h, True)
            head(HEADS - 1, True, out=True)

            take_sum(9)
            act.wait_ge(*av_taken.after(HEADS - 1))
            act.wait_ge(*mix_step.after(HEADS - 1))
            halves(1)
            for m in range(10, KT):
                split((OUT0 + m + 1) // 2, (m + 1) % 2)
                for t in range(3 * (m - 10), min(3 * (m - 9), KT)):
                    act.wait_ge(*x2_sum.after(0, t + 1))
                    nc.scalar.activation(hT[:, t, :], pd[t % 6], ACT.Copy).then_inc(x2_taken.sem, 1)
                take_sum(m)

            def square(m):
                act.wait_ge(out_taken.sem, m + 1)
                act.wait_ge(sqacc_step.sem, 1 + m)
                nc.scalar.activation(sq[:], at(hTf, m), ACT.Square).then_inc(sq_made.sem, 1)

            split((OUT0 + KT) // 2, 1)
            with act.Fori(0, KT // 2) as i:
                for j in range(2):
                    split((OUT0 + KT) // 2 + i + 1, j)
                    square(2 * i + j)

            def inverse_rms(i):
                act.wait_ge(*ssum.after(i))
                nc.scalar.activation(rstd[:], pd[0], ACT.Ln, scale=1.0 / DM, bias=eps1).then_inc(rstd_step.sem, 1)
                act.wait_ge(*rstd_step.after(i, 1))
                nc.scalar.activation(rstd[:], rstd[:], ACT.Exp, scale=-0.5).then_inc(rstd_step.sem, 1)

            inverse_rms(0)
            act.wait_ge(out_taken.sem, KT)
            nc.scalar.activation(gp[:, :, 0:1], cst[:, C_ZERO:C_ZERO + 2].unsqueeze(2), ACT.Copy).then_inc(up_taken.sem, 1)
            nc.scalar.activation(gp[:, :, S + 1:S + 2], cst[:, C_ZERO:C_ZERO + 2].unsqueeze(2), ACT.Copy).then_inc(up_taken.sem, 1)
            for m in range(KT):
                act.wait_ge(*h2_step.after(0, m + 1))
                nc.scalar.activation(act_hi[:, m, :], hn2[:, m % 2, :], ACT.Identity, bias=mod[:, 48 + m:49 + m]) \
                    .then_inc(h2_hi.sem, 1)

            def chunk(c, last=False):
                base = MLP0 // 2 + MLP_PER // 2 * c
                with act.Fori(0, FC) as f:
                    n = FC * c + f
                    pair = base + 2 * f

                    def up(part):
                        act.wait_ge(unit_used.sem, 2 * pair + 2 * part + 2)
                        act.wait_ge(fconv_step.sem, 6 * n + 3 * part + 3)
                        nc.scalar.activation(gp[:, part, 1:S + 1], pw[part][:], ACT.Copy).then_inc(up_taken.sem, 1)

                    split(pair + 1, 0)
                    up(0)
                    split(pair + 1, 1)
                    act.wait_ge(fconv_step.sem, 6 * n + 9)
                    nc.scalar.activation(cv[:, 0, :], cv[:, 0, :], ACT.Silu).then_inc(fsilu.sem, 1)
                    split(pair + 2, 0)
                    up(1)
                    split(pair + 2, 1)
                    act.wait_ge(*fprod.after(n))
                    act.wait_ge(unit_used.sem, 2 * base)
                    nc.scalar.activation(at(mhf_hi, f), prod[:], ACT.Copy).then_inc(mh_hi_made.sem, 1)
                def down(m, j=None):
                    split(base + 2 * FC + m + 1, 0)
                    split(base + 2 * FC + m + 1, 1)
                    if last:
                        act.wait_ge(out_taken.sem, KT * CHUNKS + m + 1)
                        act.wait_ge(sqacc_step.sem, KT + 1 + m)
                        nc.scalar.activation(sq[:], at(hTf, m), ACT.Square).then_inc(sq_made.sem, 1)
                        if j is not None:
                            turned(m - 2, j)

                if last:
                    down(0)
                    down(1)
                    with act.Fori(1, KT // 2) as i:
                        for j in range(2):
                            down(2 * i + j, j)
                else:
                    with act.Fori(0, KT) as m:
                        down(m)

            def turned(m, j):
                act.wait_ge(fin_sum.sem, m + 1)
                nc.scalar.activation(otok[:, :, bass.ds(m * P, P)], pd[1 + j].rearrange("p (b n) -> p b n", n=P), ACT.Copy) \
                    .then_inc(fin_taken.sem, 1)

            with act.Fori(0, CHUNKS - 1) as c:
                chunk(c)
            chunk(CHUNKS - 1, last=True)
            for j in range(2):
                turned(KT - 2 + j, j)
            act.wait_ge(*ssum.after(1))
            nc.scalar.activation(nrm[:, 1, :], pd[0][:, 0:NB], ACT.Ln, scale=1.0 / DM, bias=eps1).then_inc(rstd_step.sem, 1)
            act.wait_ge(*rstd_step.after(1, 1))
            nc.scalar.activation(nrm[:, 2, :], nrm[:, 1, :], ACT.Exp, scale=-0.5).then_inc(rstd_step.sem, 1)
            act.wait_ge(*rstd_step.after(1))
            act.wait_ge(fin_taken.sem, KT)
            for b in range(NB):
                right = otok[:, b, DM // 2:DM]
                nc.scalar.activation(right, right, ACT.Identity, scale=nrm[:, 2, b:b + 1]).then_inc(scaled_a.sem, 1)

        @block.vector
        def _(dve):
            V = nc.vector

            def low(q, slot):
                dve.wait_ge(hi_made.sem, 2 * q + slot + 1)
                V.tensor_tensor(w_lo[slot][:], raw[slot][:], w_hi[slot][:].bitcast(F32), ALU.subtract).then_inc(lo_made.sem, 1)

            def s(h, j):
                low(HEAD0 // 2 + 5 * h + (j + 1) // 2, (j + 1) % 2)

            def ada_add(w, in_sem, in_val, j, k, first=False):
                dve.wait_ge(in_sem, in_val)
                if k == 0:
                    if not first:
                        dve.wait_ge(*ada_sum.after(j - 1))
                    V.tensor_scalar(ada_acc[:], w, cond[:, k:k + 1], None, ALU.mult).then_inc(ada_step.sem, 1)
                else:
                    dve.wait_ge(ada_step.sem, KT * j + k)
                    V.scalar_tensor_tensor(ada_acc[:], w, cond[:, k:k + 1], ada_acc[:], ALU.mult, ALU.add) \
                        .then_inc(ada_step.sem, 1)

            def ada_group(h, g):
                for k in (2 * g, 2 * g + 1):
                    ada_add(ada_w[k % 2][:], ada_in[k % 2], 16 * (8 * h + k // 2 + 1), 4 + h, k)

            def ada_columns(j):
                dve.wait_ge(*ada_sum.after(j))
                i = ADA_ORDER[j] if isinstance(j, int) and j < 4 else j
                V.tensor_tensor(at(mod, i, 8), pd[5][:, 0:8], at(col, i, 8), ALU.add).then_inc(ada_out.sem, 1)

            def normed(m):
                if m < KT:
                    if m == 0:
                        dve.wait_ge(*x_turned.after(0))
                    dve.wait_ge(*scale_made.after(0, 1 + m // 8))
                    if m >= 2:
                        dve.wait_ge(*hn_lo.after(0, m - 1))
                    V.tensor_scalar(hn_tmp[m % 2], x_feat[:, m, :], mod[:, 16 + m:17 + m], mod[:, m:m + 1], ALU.mult, ALU.add) \
                        .then_inc(hn_full.sem, 1)
                if m:
                    dve.wait_ge(*hn_hi.after(0, m))
                    dve.wait_ge(*hn_full.after(0, m))
                    V.tensor_tensor(act_lo[:, m - 1, :], hn_tmp[(m - 1) % 2], act_hi[:, m - 1, :].bitcast(F32), ALU.subtract) \
                        .then_inc(hn_lo.sem, 1)

            dve.wait_ge(*cond_made.after(0))
            for j in range(4):
                for k in range(KT):
                    ada_add(ada_first[k % 4], ada_in0[k % 4], 16 * (4 * j + k // 4 + 1), j, k, first=j == 0)
                    if j == 0 and k == 7:
                        dve.wait_ge(*cols_sum.after(0))
                        V.tensor_copy(col[:, 0:443], pd[0][:, 0:443]).then_inc(cols_made.sem, 1)
                        V.tensor_copy(col[:, 443:V_N], pd[1][:, 0:V_N - 443]).then_inc(cols_made.sem, 1)
                        dve.wait_ge(*cols_made.after(0))
                    if j == 2 and k >= KT - 8:
                        normed(k - 8)
                ada_columns(j)
                if j % 2:
                    half = slice(16 + 4 * (j - 1), 24 + 4 * (j - 1))
                    dve.wait_ge(ada_out.sem, j + 1)
                    V.tensor_scalar(mod[:, half], mod[:, half], 1.0, None, ALU.add).then_inc(scale_made.sem, 1)
            low(0, 0)
            low(0, 1)
            for m in range(8, KT + 1):
                normed(m)
            dve.wait_ge(*ba_split.after(0, 1))
            V.tensor_tensor(wba_lo[:], wba, wba_hi[:].bitcast(F32), ALU.subtract).then_inc(ba_split.sem, 1)
            for i in range(3):
                dve.wait_ge(lvl_in[i], 16)
                V.tensor_copy(lvl[:, 2 * i:2 * i + 2], lvl_f32[i].rearrange("p (l d n) -> p l d n", l=2, d=2)) \
                    .then_inc(lvl_made.sem, 1)

            for t in range(2):
                low(t + 1, 0)
                low(t + 1, 1)
            dve.wait_ge(*gates_made.after(0))
            dve.wait_ge(*gate_a.after(0, 1))
            dve.wait_ge(*hn_lo.after(0))
            four = lambda t: t.rearrange("p (b n) -> p b n", n=16)
            t_x, t_s = four(tmpf[:, 0:64]), four(tmpf[:, 64:128])
            g_all = gall[:, 1].rearrange("p b d h -> p b (d h)")
            V.tensor_tensor(t_x, pd[4][:, 0:128].rearrange("p (b n) -> p b n", n=32)[:, :, 16:32],
                            gates[:, 0, :].unsqueeze(1).broadcast_to([P, NB, 16]), ALU.add).then_inc(gate_v.sem, 1)
            V.tensor_scalar(gall[:, 0], gall[:, 0], 1.0, None, ALU.add).then_inc(gate_v.sem, 1)
            dve.wait_ge(*gate_v.after(0, 2))
            V.reciprocal(gall[:, 0], gall[:, 0]).then_inc(gate_v.sem, 1)
            dve.wait_ge(*gate_a.after(0, 4))
            V.scalar_tensor_tensor(g_all, t_x, 0.0, t_s, ALU.max, ALU.add).then_inc(gate_v.sem, 1)
            dve.wait_ge(*gate_v.after(0, 4))
            V.scalar_tensor_tensor(g_all, g_all, -1.0, gates[:, 1, :].unsqueeze(1).broadcast_to([P, NB, 16]),
                                   ALU.mult, ALU.mult).then_inc(gate_v.sem, 1)
            ada_group(0, 0)
            low(3, 0)
            low(3, 1)
            dve.wait_ge(*gate_a.after(0))
            V.tensor_copy(gall[:, 2], pd[3][:, 0:64]).then_inc(gate_v.sem, 1)
            V.tensor_tensor(gall[:, 4], gall[:, 0], tmpf[:, 128:192], ALU.mult).then_inc(gate_v.sem, 1)

            ada_group(0, 1)
            low(4, 0)
            low(4, 1)
            ada_group(0, 2)
            for t in range(5):
                low(HEAD0 // 2 + t + 1, 0)
                if t < KV_HEADS:
                    dve.wait_ge(*kv_rstd.after(t))
                    V.scalar_tensor_tensor(ka[:, t, :], mixed[:, 12 + t, :], col[:, V_KN:V_KN + 1], sqa, ALU.mult, ALU.mult) \
                        .then_inc(kv_step.sem, 1)
                if t < 4:
                    low(HEAD0 // 2 + t + 1, 1)
                ada_group(0, 3 + t)
                if t < KV_HEADS:
                    dve.wait_ge(*kv_rot.after(t))
                    V.tensor_tensor(rotsin, pd[1], sinT, ALU.mult).then_inc(kv_step.sem, 1)
                    V.tensor_tensor(ka[:, t, :], ka[:, t, :], cosT, ALU.mult).then_inc(kv_step.sem, 1)
                    dve.wait_ge(*kv_step.after(t, 3))
                    V.tensor_tensor(ka[:, t, :], ka[:, t, :], rotsin, ALU.add).then_inc(kv_step.sem, 1)
            dve.wait_ge(*pads_made.after(0))
            dve.wait_ge(*lvl_made.after(0))

            def low_halves(g):
                for t in OUT_TILES[g]:
                    dve.wait_ge(*mx_hi.after(0, 8 * g + 1 + OUT_TILES[g].index(t)))
                    V.tensor_tensor(act_lo[:, t, :], mixed[:, t, :], act_hi[:, t, :].bitcast(F32), ALU.subtract) \
                        .then_inc(mx_lo.sem, 1)

            def head(h, stream, out=False):
                def ada_next(g):
                    if not out:
                        ada_group(h + 1, g)

                ada_columns(4 + h)
                V.tensor_copy(gcur[:].rearrange("p a b d -> p (a b d)"),
                              gall[:].rearrange("p a b d h -> p (a b d) h")[:, :, bass.ds(h, 1)].squeeze(2)) \
                    .then_inc(gcur_made.sem, 1)
                dve.wait_ge(*gcur_made.after(h))
                for d in range(2):
                    V.tensor_tensor(LL[:, d], cst[:, C_CUM + d * P:C_CUM + (d + 1) * P].unsqueeze(1).broadcast_to([P, NB, P]),
                                    gcur[:, 1, :, d].unsqueeze(2).broadcast_to([P, NB, P]), ALU.mult).then_inc(gu_made.sem, 1)
                for part, tile in enumerate((8, 0, 16)):
                    dve.wait_ge(tile_taken.sem, 4 + 5 * h + part + 1)
                    w = [col[:, bass.ds(V_CONV + 24 * j + tile + h, 1)] for j in range(TAPS)]
                    V.tensor_scalar(act3[:, part, :], pre[:, part, 0:S], w[0], None, ALU.mult).then_inc(conv_step.sem, 1)
                    for j in (1, 2):
                        dve.wait_ge(*conv_step.after(h, 3 * part + j))
                        V.scalar_tensor_tensor(act3[:, part, :], pre[:, part, j:j + S], w[j], act3[:, part, :],
                                               ALU.mult, ALU.add).then_inc(conv_step.sem, 1)
                    if stream and part == 1:
                        s(h + 1, 0)
                if out:
                    low_halves(0)
                dve.wait_ge(*gc_sum.after(h))
                dve.wait_ge(*eg_done.after(h))
                for d in range(2):
                    V.tensor_tensor(LL[:, d], pd[3 + d].rearrange("p (b n) -> p b n", n=P),
                                    gcur[:, 2, :, d].unsqueeze(2).broadcast_to([P, NB, P]), ALU.subtract) \
                        .then_inc(diff_made.sem, 1)
                dve.wait_ge(*diff_made.after(h))
                masks = [cst[:, c:c + 2 * P].rearrange("p (d n) -> p d n", n=P).unsqueeze(2).broadcast_to([P, 2, NB, P])
                         for c in (C_MQ, C_ML)]
                V.tensor_tensor(DQ[:], LL[:], masks[0], ALU.subtract).then_inc(dq_masked.sem, 1)
                V.tensor_tensor(LL[:], LL[:], masks[1], ALU.add).then_inc(ll_masked.sem, 1)
                if stream:
                    s(h + 1, 1)
                for i in range(2):
                    dve.wait_ge(*rstd_made.after(h, i + 1))
                    V.tensor_tensor(act3[:, i, :], act3[:, i, :], tmp[:, i, :], ALU.mult).then_inc(norm_made.sem, 1)
                dve.wait_ge(*rstd_made.after(h))
                V.scalar_tensor_tensor(qr, at(mixedf, h), col[:, V_QN:V_QN + 1], sqa, ALU.mult, ALU.mult) \
                    .then_inc(norm_made.sem, 1)
                dve.wait_ge(*rot_sum.after(h))
                V.tensor_tensor(rotsin, pd[1], sinT, ALU.mult).then_inc(rot_scaled.sem, 1)
                V.tensor_tensor(qr, qr, cosT, ALU.mult).then_inc(rope_step.sem, 1)
                dve.wait_ge(*rot_scaled.after(h))
                dve.wait_ge(*rope_step.after(h, 1))
                V.tensor_tensor(qr, qr, rotsin, ALU.add).then_inc(rope_step.sem, 1)
                if stream:
                    s(h + 1, 2)
                both = lambda t: t.unsqueeze(1).broadcast_to([P, 2, S])
                side = lambda t: t.rearrange("p (d n) -> p d n", n=S)
                factor = lambda i: gcur[:, i].rearrange("p b d -> p d b").unsqueeze(3).broadcast_to([P, 2, NB, P])
                dve.wait_ge(*decay_done.after(h, 1))
                dve.wait_ge(*g_sum.after(h))
                V.tensor_tensor(side(LLf), both(pd[5]), side(LLf), ALU.mult).then_inc(ll_step.sem, 1)
                dve.wait_ge(*ll_step.after(h, 1))
                V.tensor_tensor(LL[:], LL[:], factor(0), ALU.mult).then_inc(ll_step.sem, 1)
                dve.wait_ge(*decay_done.after(h))
                dve.wait_ge(*qk_sum.after(h))
                V.tensor_tensor(side(DQf), both(pd[0]), side(DQf), ALU.mult).then_inc(qk_made.sem, 1)
                if stream:
                    ada_next(0)

                def score_max(b):
                    dve.wait_ge(*sc_sum.after(h, b + 1))
                    n = SOFT_MAX[b] - 2
                    V.tensor_reduce(soft[:, 0, b:b + 1], pd[2 - b % 2], AX.X, ALU.max).then_inc(soft_step.sem, 1)
                    dve.wait_ge(soft_step.sem, 16 * h + n + 1)
                    V.tensor_scalar(soft[:, 1, b:b + 1], soft[:, 0, b:b + 1], -SCALE, None, ALU.mult).then_inc(soft_step.sem, 1)

                def score_norm(b):
                    dve.wait_ge(*p_exp.after(h, b + 1))
                    n = SOFT_OUT[b] - 2
                    V.reciprocal(soft[:, 3, b:b + 1], soft[:, 2, b:b + 1]).then_inc(soft_step.sem, 1)
                    dve.wait_ge(soft_step.sem, 16 * h + n + 1)
                    V.tensor_scalar(prob[b % 2], prob[b % 2], soft[:, 3, b:b + 1], None, ALU.mult).then_inc(soft_step.sem, 1)

                score_max(0)
                score_max(1)
                score_norm(0)
                score_max(2)
                score_norm(1)
                if stream:
                    s(h + 1, 3)
                score_max(3)
                score_norm(2)
                score_norm(3)
                if stream:
                    ada_next(1)
                dve.wait_ge(*tok_done.after(h, 1))
                V.tensor_tensor(tmpf.rearrange("p (d b n) -> p d b n", d=2, b=NB),
                                ktok[:].unsqueeze(1).broadcast_to([P, 2, NB, P]), factor(3), ALU.mult).then_inc(kd_made.sem, 1)
                V.tensor_copy(glast[:, 0, :], EG[:, 0, :].rearrange("p (c n) -> p c n", n=DN)[:, :, DN - 1]).then_inc(gl_made.sem, 1)
                V.tensor_copy(glast[:, 1, :], EG[:, 1, :].rearrange("p (c n) -> p c n", n=DN)[:, :, 0]).then_inc(gl_made.sem, 1)
                dve.wait_ge(*gl_made.after(h))
                V.tensor_tensor(EG[:], EG[:], both(act3[:, 1, :]), ALU.mult).then_inc(qd_made.sem, 1)
                dve.wait_ge(*av_sum.after(h))
                V.tensor_scalar(at(mixedf, h), pd[2], 1.0, None, ALU.mult).then_inc(av_taken.sem, 1)
                if stream:
                    s(h + 1, 4)
                eye = ident.unsqueeze(1).broadcast_to([P, 2 * NB, P])
                eight = lambda t: t.rearrange("p (a n) -> p a n", n=P)
                dve.wait_ge(*lm_made.after(h, 1))
                V.tensor_tensor(eight(Tf), eye, eight(LMf), ALU.subtract).then_inc(t_first.sem, 1)
                dve.wait_ge(*lt_sum.after(h))
                V.tensor_tensor(eight(TTf), eye, eight(pd01), ALU.subtract).then_inc(t_first.sem, 1)
                if stream:
                    ada_next(2)
                for n in range(1, LEVELS):
                    if n < LEVELS - 1:
                        dve.wait_ge(*a_sum.after(h, 2 * n))
                        V.tensor_tensor(Tf, Tf, pd23, ALU.subtract).then_inc(t_step.sem, 1)
                    dve.wait_ge(*a_sum.after(h, min(2 * n, 9)))
                    V.tensor_tensor(TTf, TTf, pd45, ALU.subtract).then_inc(t_step.sem, 1)
                    if stream and n < LEVELS - 1:
                        s(h + 1, 4 + n)
                        ada_next(2 + n)
                dve.wait_ge(*t_step.after(h))
                V.tensor_tensor(T[:], TT[:], factor(0), ALU.mult).then_inc(tb_made.sem, 1)
                V.tensor_tensor(TT[:], TT[:], factor(4), ALU.mult).then_inc(tb_made.sem, 1)
                if stream:
                    s(h + 1, 3 + LEVELS)
                dve.wait_ge(*wt_sum.after(h))
                V.tensor_copy(Yf, pd23).then_inc(wt_taken.sem, 1)
                dve.wait_ge(*u_taken.after(h))
                for c in range(NCH):
                    for d in range(2):
                        if c:
                            n = 2 * (c - 1) + d
                            cc = c if d == 0 else NCH - 1 - c
                            r = slice(DN * (cc % 2), DN * (cc % 2) + DN)
                            dve.wait_ge(*vn_sum.after(h, n + 1))
                            V.tensor_tensor(vn[r, d, :], LL[r, d, cc // 2, :], pd[d][r, 0:P], ALU.subtract) \
                                .then_inc(vnew_made.sem, 1)
                    for d in range(2):
                        if c < NCH - 1:
                            cc = c if d == 0 else NCH - 1 - c
                            dve.wait_ge(*s_sum.after(h, 2 * c + d + 1))
                            if c == 0:
                                V.tensor_copy(st[:, d, :], pd[d][:, P:2 * P]).then_inc(state_made.sem, 1)
                            else:
                                dve.wait_ge(*state_made.after(h, 2 * (c - 1) + d + 1))
                                V.scalar_tensor_tensor(st[:, d, :], st[:, d, :], glast[:, d, cc:cc + 1], pd[d][:, P:2 * P],
                                                       ALU.mult, ALU.add).then_inc(state_made.sem, 1)
                dve.wait_ge(*o_sum.after(h))
                dve.wait_ge(*o_taken.after(h))
                V.tensor_tensor(act3[:, 1, :], act3[:, 1, :], pd[5], ALU.add).then_inc(o_summed.sem, 1)
                if stream:
                    ada_next(7)
                dve.wait_ge(*onorm.after(h))
                V.scalar_tensor_tensor(act3[:, 1, :], act3[:, 1, :], col[:, V_DNW:V_DNW + 1], tmp[:, 1, :],
                                       ALU.mult, ALU.mult).then_inc(mix_step.sem, 1)
                dve.wait_ge(*mix_step.after(h, 1))
                V.tensor_tensor(at(mixedf, HEADS + h), act3[:, 1, :], at(mixedf, HEADS + h), ALU.mult).then_inc(mix_step.sem, 1)

            head(0, True)
            with dve.Fori(1, HEADS - 1) as h:
                head(h, True)
            head(HEADS - 1, True, out=True)

            low_halves(1)
            dve.wait_ge(ada_out.sem, ADA_STEPS)
            V.tensor_scalar(mod[:, 64:80], mod[:, 64:80], 1.0, None, ALU.add).then_inc(scale2_made.sem, 1)
            dve.wait_ge(*mx_lo.after(0))
            V.memset(sqacc[:], 0.0).then_inc(sqacc_step.sem, 1)

            def residual(unit_end, m, bank, gate):
                dve.wait_ge(unit_used.sem, unit_end)
                V.scalar_tensor_tensor(at(hTf, m), bank, mod[:, bass.ds(gate + m, 1)], at(hTf, m), ALU.mult, ALU.add) \
                    .then_inc(out_taken.sem, 1)

            def add_square(m):
                dve.wait_ge(sq_made.sem, m + 1)
                dve.wait_ge(sqacc_step.sem, 1 + m)
                V.tensor_tensor(sqacc[:], sqacc[:], sq[:], ALU.add).then_inc(sqacc_step.sem, 1)

            def add_sum(t):
                dve.wait_ge(*x2_taken.after(0, t + 1))
                dve.wait_ge(sums_taken.sem, t + 1)
                V.scalar_tensor_tensor(hT[:, t, :], sums[t], mod[:, 32 + t:33 + t], hT[:, t, :], ALU.mult, ALU.add) \
                    .then_inc(sums_added.sem, 1)

            for m in range(10, KT):
                low((OUT0 + m + 1) // 2, (m + 1) % 2)
                for t in range(max(0, 3 * (m - 11)), 3 * (m - 10)):
                    if t < 12:
                        add_sum(t)
            low((OUT0 + KT) // 2, 1)
            for t in range(12, KT):
                add_sum(t)
            dve.wait_ge(*sums_added.after(0))
            with dve.Fori(0, KT // 2) as i:
                for j in range(2):
                    m = 2 * i + j
                    low((OUT0 + KT) // 2 + i + 1, j)
                    residual(OUT0 + KT + m + 1, m, pw[j][:], 32)
                    add_square(m)
            dve.wait_ge(*rstd_step.after(0))
            dve.wait_ge(*scale2_made.after(0))

            def h2_low(m):
                dve.wait_ge(*h2_hi.after(0, m + 1))
                V.scalar_tensor_tensor(act_lo[:, m, :], hn2[:, m % 2, :], mod[:, 48 + m:49 + m], act_hi[:, m, :].bitcast(F32),
                                       ALU.add, ALU.subtract).then_inc(h2_lo.sem, 1)

            for m in range(KT):
                if m >= 2:
                    dve.wait_ge(*h2_lo.after(0, m - 1))
                V.scalar_tensor_tensor(hn2[:, m % 2, :], hT[:, m, :], mod[:, 64 + m:65 + m], rstd[:], ALU.mult, ALU.mult) \
                    .then_inc(h2_step.sem, 1)
                if m:
                    h2_low(m - 1)
            h2_low(KT - 1)
            V.memset(cv[:, 0, 0:1], 0.0).then_inc(fconv_step.sem, 3)
            V.memset(cv[:, 1, 0:1], 0.0).then_inc(fconv_step.sem, 3)

            def chunk(c, last=False):
                base = MLP0 // 2 + MLP_PER // 2 * c
                with dve.Fori(0, FC) as f:
                    n = FC * c + f
                    pair = base + 2 * f

                    def convolve(part):
                        w = [col[:, bass.ds(V_FCONV + 2 * FT * j + part * FT + n, 1)] for j in range(TAPS)]
                        bias = col[:, bass.ds(V_FB + part * FT + n, 1)]
                        dve.wait_ge(up_taken.sem, 2 * n + part + 3)
                        V.tensor_scalar(cv[:, part, :], gp[:, part, 0:S], w[0], bias, ALU.mult, ALU.add) \
                            .then_inc(fconv_step.sem, 1)
                        for j in (1, 2):
                            dve.wait_ge(fconv_step.sem, 6 * n + 6 + 3 * part + j)
                            V.scalar_tensor_tensor(cv[:, part, :], gp[:, part, j:j + S], w[j], cv[:, part, :], ALU.mult, ALU.add) \
                                .then_inc(fconv_step.sem, 1)

                    low(pair + 1, 0)
                    convolve(0)
                    low(pair + 1, 1)
                    low(pair + 2, 0)
                    convolve(1)
                    low(pair + 2, 1)
                    dve.wait_ge(*fsilu.after(n))
                    dve.wait_ge(*fconv_step.after(n + 1))
                    V.tensor_tensor(prod[:], cv[:, 0, :], cv[:, 1, :], ALU.mult).then_inc(fprod.sem, 1)
                    dve.wait_ge(*mh_hi_made.after(n))
                    V.tensor_tensor(at(mhf_lo, f), prod[:], at(mhf_hi, f).bitcast(F32), ALU.subtract) \
                        .then_inc(mh_lo_made.sem, 1)

                def down(m, j, reused=True):
                    low(base + 2 * FC + m + 1, 0)
                    low(base + 2 * FC + m + 1, 1)
                    residual(2 * base + 4 * FC + 2 * m + 2, m, pw[j][:], 80)
                    if last:
                        dve.wait_ge(sq_made.sem, KT + m + 1)
                        dve.wait_ge(sqacc_step.sem, KT + 1 + m)
                        V.tensor_tensor(sqacc[:], sqacc[:], sq[:], ALU.add).then_inc(sqacc_step.sem, 1)
                        if reused:
                            dve.wait_ge(fin_sum.sem, m - 1)
                        dve.wait_ge(out_taken.sem, KT * CHUNKS + m + 1)
                        V.tensor_scalar(hn2[:, j, :], at(hTf, m), col[:, bass.ds(V_FN + m, 1)], None, ALU.mult) \
                            .then_inc(fin_made.sem, 1)

                if last:
                    down(0, 0, reused=False)
                    down(1, 1, reused=False)
                with dve.Fori(1 if last else 0, KT // 2) as i:
                    for j in range(2):
                        down(2 * i + j, j)

            with dve.Fori(0, CHUNKS - 1) as c:
                chunk(c)
            V.memset(sqacc[:], 0.0).then_inc(sqacc_again.sem, 1)
            dve.wait_ge(*sqacc_again.after(0))
            chunk(CHUNKS - 1, last=True)
            dve.wait_ge(*rstd_step.after(1))
            dve.wait_ge(fin_taken.sem, KT)
            for b in range(NB):
                left = otok[:, b, 0:DM // 2]
                V.tensor_scalar(left, left, nrm[:, 2, b:b + 1], None, ALU.mult).then_inc(scaled_v.sem, 1)

        @block.tensor
        def _(pe):
            M, TR = pe.matmul, pe.transpose

            def out_part(g, q, slot, ks):
                if ks[0] == 0:
                    pe.wait_ge(lo_made.sem, 2 * q + slot + 1)
                for k in ks:
                    t = OUT_TILES[g][k]
                    M(pw[slot][:], w_hi[slot][:, k, :], act_hi[:, t, :], start=k == 0, stop=False)
                    M(pw[slot][:], w_hi[slot][:, k, :], act_lo[:, t, :], start=False, stop=False)
                    ins = M(pw[slot][:], w_lo[slot][:, k, :], act_hi[:, t, :], start=False, stop=k == UK - 1)
                if ks[-1] == UK - 1:
                    ins.then_inc(unit_used.sem, 1)

            def part(q, slot, ks, bank, n_k=UK, k0=None, hi=act_hi, lo=act_lo, ready=None):
                k0 = slot * UK if k0 is None else k0
                ks = range(n_k) if ks is None else ks
                if ks[0] == 0:
                    pe.wait_ge(lo_made.sem, 2 * q + slot + 1)
                for k in ks:
                    if ready:
                        pe.wait_ge(*ready(k0 + k))
                    first, last = slot == 0 and k == 0, slot == 1 and k == n_k - 1
                    M(bank, w_hi[slot][:, k, :], hi[:, k0 + k, :], start=first, stop=False)
                    M(bank, w_hi[slot][:, k, :], lo[:, k0 + k, :], start=False, stop=False)
                    ins = M(bank, w_lo[slot][:, k, :], hi[:, k0 + k, :], start=False, stop=last)
                if ks[-1] == n_k - 1:
                    ins.then_inc(unit_used.sem, 1)

            def stream(h, a, b):
                while a < b:
                    j, k = divmod(a, UK)
                    t, end = j // 2, min(b - j * UK, UK)
                    if j % 2 == 0 and k == 0:
                        pe.wait_ge(tile_taken.sem, 4 + 5 * h + t - (1 if t else 0))
                    part(HEAD0 // 2 + 5 * h + t, j % 2, range(k, end), pw[t % 2][:])
                    a = j * UK + end

            def turn_back(m, j):
                pe.wait_ge(fin_made.sem, m + 1)
                for b in range(NB):
                    ins = TR(pd[1 + j][:, b * P:(b + 1) * P], hn2[:, j, b * P:(b + 1) * P], ident)
                ins.then_inc(fin_sum.sem, 1)

            def whole(q, bank, n_k=(UK, UK), hi=act_hi, lo=act_lo, ready=None):
                part(q, 0, None, bank, n_k=n_k[0], k0=0, hi=hi, lo=lo, ready=ready)
                part(q, 1, None, bank, n_k=n_k[1], k0=n_k[0], hi=hi, lo=lo, ready=ready)

            pe.wait_ge(consts_in, 16)
            pe.wait_ge(c_in, 16)
            TR(pd[3][:, 0:KT], rows[0:KT, 5, :], ident[0:KT, 0:KT]).then_inc(c_sum.sem, 1)
            pe.wait_ge(rows_in, 16 * 10)
            at_col = 0
            for i, n in enumerate((115, 72, 128, 128, 96)):
                bank, c0 = (0, at_col) if i < 4 else (1, at_col - 443)
                ins = TR(pd[bank][:, c0:c0 + n], rows[0:n, i, :], ident[0:n, 0:n])
                at_col += n
            ins.then_inc(cols_sum.sem, 1)
            pe.wait_ge(small_in, 32)
            M(pd[2][:, 0:32], ones[0:1, :], arow, start=True, stop=True).then_inc(gate_row_sum.sem, 1)

            def ada_sums(j):
                pe.wait_ge(*ada_step.after(j))
                for i in range(8):
                    ins = M(pd[5][:, i:i + 1], ada_acc[:, i * P:(i + 1) * P], ones[:, 0:1], start=True, stop=True)
                ins.then_inc(ada_sum.sem, 1)

            ada_sums(0)
            pe.wait_ge(*x_normed.after(0))
            pe.wait_ge(*gates_made.after(0))
            pe.wait_ge(*cols_made.after(0))
            for m in range(KT):
                if m >= 4:
                    pe.wait_ge(*x_turned.after(0, m - 3))
                for b in range(NB):
                    ins = TR(pd[m % 4][:, b * P:(b + 1) * P], x_in[:, b, m * P:(m + 1) * P], ident)
                ins.then_inc(xt_sum.sem, 1)
            for j in range(1, 4):
                pe.wait_ge(*ada_out.after(j - 1))
                ada_sums(j)
            whole(0, pw[0][:], ready=lambda k: hn_lo.after(0, k + 1))
            pe.wait_ge(*ba_split.after(0))
            for k in range(KT):
                for i, (w, t) in enumerate(((wba_hi, act_hi), (wba_hi, act_lo), (wba_lo, act_hi))):
                    ins = M(pd[4][0:32, :], w[:, k, :], t[:, k, :], start=k == 0 and i == 0, stop=k == KT - 1 and i == 2)
            ins.then_inc(ba_row_sum.sem, 1)
            whole(1, pw[1][:])
            pe.wait_ge(*ba_row_taken.after(0))
            for b in range(NB):
                ins = TR(pd[4][:, b * 32:(b + 1) * 32], tmp[0:32, 0, b * P:(b + 1) * P], ident[0:32, 0:32])
            ins.then_inc(ba_sum.sem, 1)
            pe.wait_ge(tile_taken.sem, 1)
            whole(2, pw[0][:])
            pe.wait_ge(more_in, 16)
            pe.wait_ge(*gate_v.after(0, 5))
            for i, c0 in enumerate((C_CUM, C_REST)):
                for b in range(NB):
                    for d in range(2):
                        o = i * 64 + b * 16 + d * 8
                        ins = M(pd[3][:, o:o + 8], cst[:, c0 + d * P:c0 + (d + 1) * P], gall[:, 1, b, d, :], start=True, stop=True)
            ins.then_inc(cum_sum.sem, 1)
            pe.wait_ge(tile_taken.sem, 2)
            whole(3, pw[1][:])
            pe.wait_ge(*gate_v.after(0))
            for j in range(10):
                stream(0, UK * j, UK * (j + 1))
                g = j // 2
                if g < KV_HEADS and j % 2:
                    pe.wait_ge(*kv_sq.after(g))
                    M(pd[2], ones, sqa, start=True, stop=True).then_inc(kv_ss.sem, 1)
                    if g:
                        pe.wait_ge(*v_tok.after(g - 1))
                    for b in range(NB):
                        ins = TR(pd[3][:, b * P:(b + 1) * P], mixed[:, 14 + g, b * P:(b + 1) * P], ident)
                    ins.then_inc(v_tr.sem, 1)
                if j in (2, 4):
                    g = j // 2 - 1
                    pe.wait_ge(kv_step.sem, 4 * g + 1)
                    M(pd[1], rot, ka[:, g, :], start=True, stop=True).then_inc(kv_rot.sem, 1)
            pe.wait_ge(*v_tok.after(1))
            pe.wait_ge(*kv_step.after(1))

            def head(h, first=False, out=False):
                def run(a, b):
                    if not out:
                        stream(h + 1, a, b)
                        return
                    if a == 0:
                        return
                    if a == 4:
                        pe.wait_ge(*mx_lo.after(0, 8))
                        a = 0
                    while a < b:
                        m, k = divmod(a, UK)
                        end = min(b - m * UK, UK)
                        if k == 0 and m >= 2:
                            pe.wait_ge(sums_taken.sem, m - 1)
                        elif k == 0:
                            pe.wait_ge(tile_taken.sem, 4 + 5 * HEADS)
                        out_part(0, OUT0 // 2 + m // 2, m % 2, range(k, end))
                        a = m * UK + end

                blk = lambda t, b: t[:, b * P:(b + 1) * P]
                ada_sums(4 + h)
                run(0, 4)
                pe.wait_ge(*gu_made.after(h))
                if not first:
                    pe.wait_ge(*o_taken.after(h - 1))
                for d in range(2):
                    M(pd[3 + d], ones, LL[:, d].rearrange("p b n -> p (b n)"), start=True, stop=True).then_inc(gc_sum.sem, 1)
                run(4, 12)
                if not first:
                    pe.wait_ge(*mix_step.after(h - 1))
                for i, t in enumerate((tmp[:, 0, :], tmp[:, 1, :], sqa)):
                    pe.wait_ge(*sq_done.after(h, i + 1))
                    M(pd[i], ones, t, start=True, stop=True).then_inc(ss_sum.sem, 1)
                run(12, 20)
                k_f, q_f, v_f = act3[:, 0, :], act3[:, 1, :], act3[:, 2, :]
                pe.wait_ge(*norm_made.after(h, 3))
                M(pd[1], rot, qr, start=True, stop=True).then_inc(rot_sum.sem, 1)
                pe.wait_ge(*ada_out.after(4 + h))
                for b in range(NB):
                    ins = M(blk(pd[5], b), blk(k_f, b), blk(k_f, b), start=True, stop=True)
                ins.then_inc(g_sum.sem, 1)
                for b in range(NB):
                    ins = M(blk(pd[0], b), blk(k_f, b), blk(q_f, b), start=True, stop=True)
                ins.then_inc(qk_sum.sem, 1)
                pe.wait_ge(*diff_made.after(h))
                pe.wait_ge(*silu_done.after(h, 3))
                for bank, t in ((pd[3], k_f), (pd[4], v_f)):
                    for b in range(NB):
                        ins = TR(blk(bank, b), blk(t, b), ident)
                    ins.then_inc(tr_sum.sem, 1)
                run(20, 22)

                def scores(b):
                    M(pd[2 - b % 2], blk(qr, b), group(ka, h), start=True, stop=True).then_inc(sc_sum.sem, 1)

                def turn(b):
                    pe.wait_ge(soft_step.sem, 16 * h + SOFT_OUT[b])
                    if b >= 2:
                        pe.wait_ge(*pt_taken.after(h, b - 1))
                    for k in range(NB):
                        ins = TR(blk(pd[3 + b % 2], k), blk(prob[b % 2], k), ident)
                    ins.then_inc(pt_sum.sem, 1)

                pe.wait_ge(*rope_step.after(h))
                scores(0)
                scores(1)
                run(22, 28)
                pe.wait_ge(*tok_done.after(h))
                pe.wait_ge(*p_exp.after(h, 1))
                scores(2)
                turn(0)
                pe.wait_ge(*p_exp.after(h, 2))
                scores(3)
                turn(1)
                run(28, 32)
                turn(2)
                turn(3)
                run(32, 36)
                pe.wait_ge(*pt_taken.after(h))
                pe.wait_ge(*vcur_made.after(h))
                for k in range(NB):
                    ins = M(pd[2], vcur[:, k, :], PT[:, k, :], start=k == 0, stop=k == NB - 1)
                ins.then_inc(av_sum.sem, 1)
                run(36, 38)
                pe.wait_ge(*lm_made.after(h, 1))
                pe.wait_ge(*qk_made.after(h))
                eight = [(d, b) for d in range(2) for b in range(NB)]
                p8 = lambda t, i: t[:, i * P:(i + 1) * P]
                for i in range(8):
                    ins = TR(p8(pd01, i), p8(LMf, i), ident)
                ins.then_inc(lt_sum.sem, 1)
                run(38, 42)
                for n in range(1, LEVELS):
                    pe.wait_ge(*lm_made.after(h, n + 1))
                    if n == 1:
                        pe.wait_ge(*t_first.after(h))
                    else:
                        pe.wait_ge(*t_step.after(h, 2 * (n - 1)))
                    for i in range(8):
                        ins = M(p8(pd01, i), p8(LMf, i), p8(TTf, i), start=True, stop=True)
                    ins.then_inc(y_sum.sem, 1)
                    run(36 + 6 * n, 38 + 6 * n)
                    pe.wait_ge(*y_taken.after(h, n))
                    if n == 1:
                        pe.wait_ge(*av_taken.after(h))
                    if n < LEVELS - 1:
                        for i in range(8):
                            ins = M(p8(pd23, i), p8(Yf, i), p8(Tf, i), start=True, stop=True)
                        ins.then_inc(a_sum.sem, 1)
                    for i in range(8):
                        ins = M(p8(pd45, i), p8(Tf, i), p8(Yf, i), start=True, stop=True)
                    ins.then_inc(a_sum.sem, 1)
                    run(38 + 6 * n, 42 + 6 * n)
                run(72, 74)
                pe.wait_ge(*tb_made.after(h, 1))
                for i, (d, b) in enumerate(eight):
                    ins = M(p8(pd01, i), p8(Tf, i), vtok[:, b, :], start=True, stop=True)
                ins.then_inc(u_sum.sem, 1)
                pe.wait_ge(*tb_made.after(h))
                for i, (d, b) in enumerate(eight):
                    ins = M(p8(pd23, i), ktok[:, b, :], p8(TTf, i), start=True, stop=True)
                ins.then_inc(wt_sum.sem, 1)
                run(74, 76)
                pe.wait_ge(*u_taken.after(h))
                pe.wait_ge(*wt_taken.after(h))
                pe.wait_ge(*kd_made.after(h))
                pe.wait_ge(*qd_made.after(h))
                for c in range(NCH):
                    for d in range(2):
                        if c:
                            cc = c if d == 0 else NCH - 1 - c
                            i, r0 = d * NB + cc // 2, DN * (cc % 2)
                            pe.wait_ge(*state_made.after(h, 2 * (c - 1) + d + 1))
                            M(pd[d][r0:r0 + DN, 0:P], Yf[:, i * P + r0:i * P + r0 + DN], st[:, d, :], start=True, stop=True) \
                                .then_inc(vn_sum.sem, 1)
                    if 1 <= c <= 4:
                        run(75 + c, 76 + c)
                    for d in range(2):
                        cc = c if d == 0 else NCH - 1 - c
                        i, r0 = d * NB + cc // 2, DN * (cc % 2)
                        r = slice(r0, r0 + DN)
                        o = pd[4 + d][:, cc * DN:(cc + 1) * DN]
                        if c:
                            new = vn[r, d, :]
                            pe.wait_ge(*vnew_made.after(h, 2 * (c - 1) + d + 1))
                            M(o, st[:, d, :], EG[:, d, cc * DN:(cc + 1) * DN], start=True, stop=False)
                        else:
                            new = LLf[r, i * P:(i + 1) * P]
                        ins = M(o, new, DQf[r, i * P + r0:i * P + r0 + DN], start=c == 0, stop=True)
                        if c == NCH - 1:
                            ins.then_inc(o_sum.sem, 1)
                        else:
                            M(pd[d][:, P:2 * P], tmpf[r, i * P:(i + 1) * P], new, start=True, stop=True).then_inc(s_sum.sem, 1)
                pe.wait_ge(*onorm.after(h, 1))
                M(pd[2], ones, tmp[:, 0, :], start=True, stop=True).then_inc(sso_sum.sem, 1)

            head(0, first=True)
            with pe.Fori(1, HEADS - 1) as h:
                head(h)
            head(HEADS - 1, out=True)

            for m in range(10, KT):
                pe.wait_ge(sums_taken.sem, m - 1)
                out_part(0, (OUT0 + m) // 2, m % 2, range(UK))
                if m == 10:
                    pe.wait_ge(*mix_step.after(HEADS - 1))
                for t in range(3 * (m - 10), min(3 * (m - 9), KT)):
                    pe.wait_ge(x2_in[t % X_SLOTS], 16 * (t // X_SLOTS + 1))
                    if t >= 6:
                        pe.wait_ge(*x2_taken.after(0, t - 5))
                    for b in range(NB):
                        ins = TR(pd[t % 6][:, b * P:(b + 1) * P], xs[:, t % X_SLOTS, b, :], ident)
                    ins.then_inc(x2_sum.sem, 1)
            pe.wait_ge(*mx_lo.after(0))
            for m in range(2):
                pe.wait_ge(sums_taken.sem, KT - 1 + m)
                out_part(1, (OUT0 + KT) // 2, m, range(UK))
            with pe.Fori(1, KT // 2) as i:
                for j in range(2):
                    pe.wait_ge(out_taken.sem, 2 * i + j - 1)
                    out_part(1, (OUT0 + KT) // 2 + i, j, range(UK))
            pe.wait_ge(sqacc_step.sem, KT + 1)
            pe.wait_ge(*x2_taken.after(0))
            M(pd[0], ones, sqacc[:], start=True, stop=True).then_inc(ssum.sem, 1)

            def chunk(c, first=False, last=False):
                base = MLP0 // 2 + MLP_PER // 2 * c

                def up(f, ready=None):
                    for j in range(2):
                        pe.wait_ge(out_taken.sem, KT * (c + 1) - 1 + j)
                        pe.wait_ge(up_taken.sem, 2 * (FC * c + f) + j + 1)
                        whole(base + 2 * f + j, pw[j][:], ready=ready if j == 0 else None)

                def down(m, j):
                    q, bank = base + 2 * FC + m, pw[j][:]
                    pe.wait_ge(up_taken.sem, 2 * FC * (c + 1) + 1 + j)
                    pe.wait_ge(out_taken.sem, KT * (c + 1) + m - 1)
                    pe.wait_ge(mh_lo_made.sem, FC * c + 6)
                    part(q, 0, None, bank, n_k=6, k0=0, hi=mh_hi, lo=mh_lo)
                    part(q, 1, None, bank, n_k=FC - 6, k0=6, hi=mh_hi, lo=mh_lo, ready=lambda k: (mh_lo_made.sem, FC * c + k + 1))

                if first:
                    up(0, ready=lambda k: h2_lo.after(0, k + 1))
                with pe.Fori(1 if first else 0, FC) as f:
                    up(f)
                if last:
                    down(0, 0)
                    down(1, 1)
                with pe.Fori(1 if last else 0, KT // 2) as i:
                    for j in range(2):
                        down(2 * i + j, j)
                        if last:
                            turn_back(2 * i + j - 2, j)

            chunk(0, first=True)
            with pe.Fori(1, CHUNKS - 1) as c:
                chunk(c)
            chunk(CHUNKS - 1, last=True)
            for j in range(2):
                pe.wait_ge(fin_taken.sem, KT - 3 + j)
                turn_back(KT - 2 + j, j)
            pe.wait_ge(sqacc_step.sem, 2 * KT + 1)
            for b in range(NB):
                ins = M(pd[0][:, b:b + 1], sqacc[:, b * P:(b + 1) * P], ones[:, 0:1], start=True, stop=True)
            ins.then_inc(ssum.sem, 1)


_INS = ["x", "c", "w_ada", "b_ada", "w_in", "attn_q_norm", "attn_k_norm", "dn_conv_w", "dn_A_log", "dn_dt_bias",
        "dn_norm_w", "w_out", "w_up", "w_ffn_conv", "b_ffn_conv", "w_down", "final_norm"]


def kernel(**inputs):
    import numpy as np
    import concourse.bacc as bacc
    from concourse.bass_utils import run_bass_kernel_spmd

    nc = bacc.Bacc("TRN2", target_bir_lowering=False, num_devices=1)
    arrays = {name: np.ascontiguousarray(inputs[name]) for name in _INS}
    constants, levels = shape_constants(np)
    arrays["shape_constants"], arrays["level_masks"] = constants, levels
    aps, in_map = {}, {}
    for name, a in arrays.items():
        in_map[f"in_{name}_dram"] = a
        aps[name] = nc.dram_tensor(f"in_{name}_dram", a.shape, mybir.dt.from_np(a.dtype), kind="ExternalInput").ap()
    out = nc.dram_tensor("out_dram", (1, S, DM), F32, kind="ExternalOutput").ap()
    build(nc, aps, out)
    r = run_bass_kernel_spmd(nc, [in_map], core_ids=[0])
    return r.results[0]["out_dram"]
```
